# Optimizing a Trainium2 kernel written in Bass

```python
import math
import jax, jax.numpy as jnp
from jax import lax
import numpy as np

D_MODEL = 1024
BATCH = 1
SEQ = 128
DEPTH = 1
DEC_BATCH = 1
DEC_SEQ = 128
PAST_LEN = 128

GRID_W = 64
EPS = 1e-6
SSM_WIDTH = D_MODEL // 2
SSM_GROUP = 16
SSM_GROUPS = SSM_WIDTH // SSM_GROUP
SSM_STATE = 64
MLA_HEADS = 8
QK_NOPE = 64
QK_ROPE = 32
V_DIM = 64
Q_RANK = 384
KV_RANK = 256
MLA_WIDTH = MLA_HEADS * V_DIM
MIX_WIDTH = SSM_WIDTH + MLA_WIDTH
IN_WIDTH = SSM_WIDTH + Q_RANK + KV_RANK + QK_ROPE
IN_SPLITS = (SSM_WIDTH, SSM_WIDTH + Q_RANK, SSM_WIDTH + Q_RANK + KV_RANK)
ROPE_BASE = 10000.0
Q_BLOCK = 128
N_KEYS = 128
N_EXPERTS = N_KEYS * N_KEYS
PEER_HEADS = 8
PEER_TOPK = 16
KEY_DIM = 128
TOKEN_BLOCK = 128

kernel_name = "hymba_s5_mla_peer_prefix_dit"

F32 = jnp.float32

def rmsnorm(x, g):
    xf = x.astype(F32)
    y = xf * lax.rsqrt(jnp.mean(xf * xf, axis=-1, keepdims=True) + EPS)
    return (y * g.astype(F32)).astype(x.dtype)

def modulation(cvec, w_mod, b_mod):
    m = jax.nn.silu(cvec) @ w_mod + b_mod
    return jnp.split(m[..., None, :], 6, axis=-1)

def modulate(x, g, shift, scale):
    return rmsnorm(x, g) * (1 + scale) + shift

def axial_rope_tables(n_tokens):
    n_rows = n_tokens // GRID_W
    rows = jnp.repeat(jnp.arange(n_rows, dtype=F32), GRID_W)
    cols = jnp.tile(jnp.arange(GRID_W, dtype=F32), n_rows)
    half = QK_ROPE // 2
    inv_freq = 1.0 / (ROPE_BASE ** (jnp.arange(0, half, 2, dtype=F32) / half))
    ang_r = rows[:, None] * inv_freq
    ang_c = cols[:, None] * inv_freq
    ang = jnp.concatenate([ang_r, ang_r, ang_c, ang_c], axis=-1)
    return jnp.cos(ang), jnp.sin(ang)

def apply_rope(x, cos, sin):
    xs = x.reshape(x.shape[:-1] + (2, 2, QK_ROPE // 4))
    rot = jnp.stack([-xs[..., 1, :], xs[..., 0, :]], axis=-2).reshape(x.shape)
    return (x * cos + rot * sin).astype(x.dtype)

def cmul(ar, ai, br, bi):
    return ar * br - ai * bi, ar * bi + ai * br

def s5_discretise(lam_re, lam_im, log_dt):
    dt = jnp.exp(log_dt.astype(F32))[:, None]
    lr, li = lam_re.astype(F32), lam_im.astype(F32)
    mag = jnp.exp(lr * dt)
    ab_re, ab_im = mag * jnp.cos(li * dt), mag * jnp.sin(li * dt)
    den = lr * lr + li * li
    f_re, f_im = cmul(ab_re - 1.0, ab_im, lr / den, -li / den)
    return ab_re, ab_im, f_re, f_im

def s5_combine(e1, e2):
    a1r, a1i, b1r, b1i = e1
    a2r, a2i, b2r, b2i = e2
    ar, ai = cmul(a2r, a2i, a1r, a1i)
    br, bi = cmul(a2r, a2i, b1r, b1i)
    return ar, ai, br + b2r, bi + b2i

def s5_scan(uf, b_re, b_im, lam_re, lam_im, log_dt, h0, reverse):
    ab_re, ab_im, f_re, f_im = s5_discretise(lam_re, lam_im, log_dt)
    bu_re = jnp.einsum('btgp,gnp->btgn', uf, b_re.astype(F32))
    bu_im = jnp.einsum('btgp,gnp->btgn', uf, b_im.astype(F32))
    bu_re, bu_im = cmul(f_re, f_im, bu_re, bu_im)
    if h0 is not None:
        h_re0, h_im0 = cmul(ab_re, ab_im, h0[0].astype(F32), h0[1].astype(F32))
        edge = -1 if reverse else 0
        bu_re = bu_re.at[:, edge].add(h_re0)
        bu_im = bu_im.at[:, edge].add(h_im0)
    a_re = jnp.broadcast_to(ab_re, bu_re.shape)
    a_im = jnp.broadcast_to(ab_im, bu_im.shape)
    _, _, h_re, h_im = lax.associative_scan(s5_combine, (a_re, a_im, bu_re, bu_im),
                                            reverse=reverse, axis=1)
    return h_re, h_im

def s5_mixer(u, p, h0_state):
    B, T, _ = u.shape
    uf = u.astype(F32).reshape(B, T, SSM_GROUPS, SSM_GROUP)
    y = uf * p['ssm_d'].astype(F32).reshape(SSM_GROUPS, SSM_GROUP)
    finals = []
    for d, reverse in ((0, False), (1, True)):
        init = None if h0_state is None else (h0_state[:, d, 0], h0_state[:, d, 1])
        h_re, h_im = s5_scan(uf, p['ssm_b_re'][d], p['ssm_b_im'][d], p['ssm_lam_re'][d],
                             p['ssm_lam_im'][d], p['ssm_log_dt'][d], init, reverse)
        y = y + (jnp.einsum('btgn,gpn->btgp', h_re, p['ssm_c_re'][d].astype(F32))
                 - jnp.einsum('btgn,gpn->btgp', h_im, p['ssm_c_im'][d].astype(F32)))
        edge = 0 if reverse else -1
        finals.append(jnp.stack([h_re[:, edge], h_im[:, edge]], axis=1))
    state = jnp.stack(finals, axis=1)
    yg = jax.nn.gelu(y.reshape(B, T, SSM_WIDTH))
    out = yg * jax.nn.sigmoid(yg @ p['w_glu'].astype(F32))
    return out.astype(u.dtype), state.astype(u.dtype)

def attend(q, k, v):
    B, T, H, dk = q.shape
    dv = v.shape[-1]
    nb = T // Q_BLOCK
    qb = q.reshape(B, nb, Q_BLOCK, H, dk).transpose(1, 0, 2, 3, 4)
    scale = dk ** -0.5

    def one_block(qblk):
        s = jnp.einsum('bqhd,bshd->bhqs', qblk, k).astype(F32) * scale
        w = jax.nn.softmax(s, axis=-1).astype(v.dtype)
        return jnp.einsum('bhqs,bshd->bqhd', w, v)

    o = lax.map(one_block, qb)
    return o.transpose(1, 0, 2, 3, 4).reshape(B, T, H * dv)

def peer(h, w_query, sub_keys, u_table, v_table):
    B, T, D = h.shape
    x = h.reshape(B * T, D)
    q = (x @ w_query).reshape(-1, PEER_HEADS, 2, KEY_DIM)
    s = jnp.einsum('nhid,hikd->nhik', q, sub_keys).astype(F32)
    top_s, top_i = lax.top_k(s, PEER_TOPK)
    cand_s = (top_s[..., 0, :, None] + top_s[..., 1, None, :]).reshape(-1, PEER_HEADS, PEER_TOPK * PEER_TOPK)
    cand_i = (top_i[..., 0, :, None] * N_KEYS + top_i[..., 1, None, :]).reshape(-1, PEER_HEADS, PEER_TOPK * PEER_TOPK)
    best_s, pos = lax.top_k(cand_s, PEER_TOPK)
    idx = jnp.take_along_axis(cand_i, pos, axis=-1)
    g = jax.nn.softmax(best_s, axis=-1)
    nblk = x.shape[0] // TOKEN_BLOCK

    def one_block(args):
        xb, ib, gb = args
        act = jax.nn.gelu(jnp.einsum('nd,nhkd->nhk', xb, u_table[ib]).astype(F32)) * gb
        return jnp.einsum('nhk,nhkd->nd', act.astype(xb.dtype), v_table[ib])

    out = lax.map(one_block, (x.reshape(nblk, TOKEN_BLOCK, D),
                              idx.reshape(nblk, TOKEN_BLOCK, PEER_HEADS, PEER_TOPK),
                              g.reshape(nblk, TOKEN_BLOCK, PEER_HEADS, PEER_TOPK)))
    return out.reshape(B, T, D)

def trunk_layer(x, cvec, p, rope=None, ctx=None):
    B, T, _ = x.shape
    sh1, sc1, g1, sh2, sc2, g2 = modulation(cvec, p['w_mod'], p['b_mod'])
    h = modulate(x, p['norm1'], sh1, sc1)
    u, c_q, c_kv, k_rope = jnp.split(h @ p['w_in'], IN_SPLITS, axis=-1)
    ssm_out, ssm_state = s5_mixer(u, p, None if ctx is None else ctx[2])
    q = (rmsnorm(c_q, p['q_norm']) @ p['w_uq']).reshape(B, T, MLA_HEADS, QK_NOPE + QK_ROPE)
    ckv = rmsnorm(c_kv, p['kv_norm'])
    if ctx is None:
        ckv_all, krope_all = ckv, k_rope
    else:
        cos, sin = rope
        q = jnp.concatenate([q[..., :QK_NOPE],
                             apply_rope(q[..., QK_NOPE:], cos[:, None, :], sin[:, None, :])], axis=-1)
        ckv_all = jnp.concatenate([ctx[0].astype(ckv.dtype), ckv], axis=1)
        krope_all = jnp.concatenate([ctx[1].astype(k_rope.dtype), apply_rope(k_rope, cos, sin)], axis=1)
    S = ckv_all.shape[1]
    k_nope = (ckv_all @ p['w_uk']).reshape(B, S, MLA_HEADS, QK_NOPE)
    v = (ckv_all @ p['w_uv']).reshape(B, S, MLA_HEADS, V_DIM)
    k = jnp.concatenate([k_nope, jnp.broadcast_to(krope_all[:, :, None, :], (B, S, MLA_HEADS, QK_ROPE))], axis=-1)
    attn = attend(q, k, v)
    mix = jnp.concatenate([ssm_out, attn], axis=-1) @ p['w_out']
    x = x + g1 * mix
    h2 = modulate(x, p['norm2'], sh2, sc2)
    x = x + g2 * peer(h2, p['w_query'], p['sub_keys'], p['u_table'], p['v_table'])
    return x, ckv, k_rope, ssm_state

def setup_inputs(seed: int = 0) -> dict:
    key = jax.random.key(seed)
    ks = list(jax.random.split(key, 40))
    cnt = [0]

    def nk():
        cnt[0] += 1
        return ks[cnt[0] - 1]

    def nrm(shape, s):
        return s * jax.random.normal(nk(), shape, F32)

    L, G, N, P, D = DEPTH, SSM_GROUPS, SSM_STATE, SSM_GROUP, D_MODEL
    return {
        'x_prompt': nrm((BATCH, SEQ, D), 1.0),
        'x_sample': nrm((DEC_BATCH, DEC_SEQ, D), 1.0),
        'c': nrm((DEC_BATCH, D), 1.0),
        'cache_ckv': nrm((DEC_BATCH, L, PAST_LEN, KV_RANK), 1.0),
        'cache_krope': nrm((DEC_BATCH, L, PAST_LEN, QK_ROPE), 1.0),
        'state_ssm': nrm((DEC_BATCH, L, 2, 2, G, N), 0.5),
        'c_ctx': nrm((D,), 1.0),
        'w_mod': nrm((L, D, 6 * D), 0.5 * D ** -0.5),
        'b_mod': nrm((L, 6 * D), 0.02),
        'norm1': 1.0 + nrm((L, D), 0.02),
        'w_in': nrm((L, D, IN_WIDTH), D ** -0.5),
        'ssm_lam_re': -0.5 + nrm((L, 2, G, N), 0.01),
        'ssm_lam_im': jnp.pi * jnp.arange(N, dtype=F32) + nrm((L, 2, G, N), 0.01),
        'ssm_log_dt': jax.random.uniform(nk(), (L, 2, G), F32, math.log(1e-3), math.log(1e-1)),
        'ssm_b_re': nrm((L, 2, G, N, P), (2 * P) ** -0.5),
        'ssm_b_im': nrm((L, 2, G, N, P), (2 * P) ** -0.5),
        'ssm_c_re': nrm((L, 2, G, P, N), (2 * N) ** -0.5),
        'ssm_c_im': nrm((L, 2, G, P, N), (2 * N) ** -0.5),
        'ssm_d': nrm((L, SSM_WIDTH), 1.0),
        'w_glu': nrm((L, SSM_WIDTH, SSM_WIDTH), SSM_WIDTH ** -0.5),
        'q_norm': 1.0 + nrm((L, Q_RANK), 0.02),
        'w_uq': nrm((L, Q_RANK, MLA_HEADS * (QK_NOPE + QK_ROPE)), Q_RANK ** -0.5),
        'kv_norm': 1.0 + nrm((L, KV_RANK), 0.02),
        'w_uk': nrm((L, KV_RANK, MLA_HEADS * QK_NOPE), KV_RANK ** -0.5),
        'w_uv': nrm((L, KV_RANK, MLA_HEADS * V_DIM), KV_RANK ** -0.5),
        'w_out': nrm((L, MIX_WIDTH, D), MIX_WIDTH ** -0.5),
        'norm2': 1.0 + nrm((L, D), 0.02),
        'w_query': nrm((L, D, PEER_HEADS * 2 * KEY_DIM), D ** -0.5),
        'sub_keys': nrm((L, PEER_HEADS, 2, N_KEYS, KEY_DIM), KEY_DIM ** -0.5),
        'u_table': nrm((L, N_EXPERTS, D), D ** -0.5),
        'v_table': nrm((L, N_EXPERTS, D), 0.5),
        'final_norm': 1.0 + nrm((D,), 0.02),
    }

def reference(x_prompt, x_sample, c, cache_ckv, cache_krope, state_ssm, c_ctx,
              w_mod, b_mod, norm1, w_in, ssm_lam_re, ssm_lam_im, ssm_log_dt,
              ssm_b_re, ssm_b_im, ssm_c_re, ssm_c_im, ssm_d, w_glu, q_norm, w_uq,
              kv_norm, w_uk, w_uv, w_out, norm2, w_query, sub_keys, u_table, v_table,
              final_norm):
    cos, sin = axial_rope_tables(x_sample.shape[1])
    yp, ys = x_prompt, x_sample
    ckv_list, krope_list, ssm_list = [], [], []
    for l in range(DEPTH):
        p = {
            'w_mod': w_mod[l], 'b_mod': b_mod[l], 'norm1': norm1[l], 'w_in': w_in[l],
            'ssm_lam_re': ssm_lam_re[l], 'ssm_lam_im': ssm_lam_im[l], 'ssm_log_dt': ssm_log_dt[l],
            'ssm_b_re': ssm_b_re[l], 'ssm_b_im': ssm_b_im[l], 'ssm_c_re': ssm_c_re[l],
            'ssm_c_im': ssm_c_im[l], 'ssm_d': ssm_d[l], 'w_glu': w_glu[l],
            'q_norm': q_norm[l], 'w_uq': w_uq[l], 'kv_norm': kv_norm[l], 'w_uk': w_uk[l],
            'w_uv': w_uv[l], 'w_out': w_out[l], 'norm2': norm2[l], 'w_query': w_query[l],
            'sub_keys': sub_keys[l], 'u_table': u_table[l], 'v_table': v_table[l],
        }
        yp, ckv_l, krope_l, ssm_l = trunk_layer(yp, c_ctx, p)
        ckv_list.append(ckv_l)
        krope_list.append(krope_l)
        ssm_list.append(ssm_l)
        ys, _, _, _ = trunk_layer(ys, c, p, rope=(cos, sin),
                                  ctx=(cache_ckv[:, l], cache_krope[:, l], state_ssm[:, l]))
    y_prompt = rmsnorm(yp, final_norm)
    y_sample = rmsnorm(ys, final_norm)
    new_ckv = jnp.stack(ckv_list, axis=1)
    new_krope = jnp.stack(krope_list, axis=1)
    new_ssm = jnp.stack(ssm_list, axis=1)
    return (y_prompt, y_sample, new_ckv, new_krope, new_ssm)


_drawn_inputs = setup_inputs


def setup_inputs(seed=0):
    import zlib

    import numpy as np

    out = dict(_drawn_inputs(seed))
    spreads = {}
    factors = {'cache_ckv': 2.805,
     'cache_krope': 4.693,
     'norm1': 2.883,
     'ssm_lam_re': 4.461,
     'q_norm': 8.0,
     'kv_norm': 3.133,
     'norm2': 4.052,
     'final_norm': 2.902}
    for name, (base, spread) in spreads.items():
        noise = np.random.default_rng([zlib.crc32(name.encode()), seed]).standard_normal(out[name].shape)
        drawn = base * np.exp(spread * noise) if base else spread * noise
        out[name] = __import__('jax').numpy.asarray(drawn.astype(out[name].dtype))
    for name, factor in factors.items():
        out[name] = (out[name] * factor).astype(out[name].dtype)
    return out
```

```python
import math
from contextlib import ExitStack

import numpy as np

import concourse.bass as bass
from concourse import mybir

F32 = mybir.dt.float32
U32 = mybir.dt.uint32
ALU = mybir.AluOpType
ACT = mybir.ActivationFunctionType
AX = mybir.AxisListType

P = 128
G = 2
D = 1024
KD = D // P
EPS = 1e-6
SSM = 512
SG, SN, SP_ = 32, 64, 16
TILES = SG * SN // P
NC = SSM // P
QR, KVR, ROPE, NOPE, VD = 384, 256, 32, 64, 64
HEADS = 8
QK = NOPE + ROPE
SCALE = QK ** -0.5
PH, TOPK, NKEYS = 8, 16, 128
HI = PH * 2
PICKS = PH * TOPK
BATCH = 8
NB = PICKS // BATCH
WSLOT = KD * 512
NSLOT = 4
MAGIC = 12582912.0
INV_2PI = 1.0 / (2.0 * math.pi)
C1 = 6.28125
C2 = 2.0 * math.pi - C1
LOW = -3.0e38

LOADS = ([f"mod{n}" for n in range(4)] + ["in_u", "in_q", "in_kv"] + [f"mod{n}" for n in range(4, 12)]
         + ["glu", "uq", "ukv", "out0", "out1"] + [f"query{n}" for n in range(4)])


def bank_plan():
    order = [(f"mod{n}", 6 + n % 2) for n in range(4)]
    order += [(f"bc_{v}_{g}_{h}", b + h) for g, bb in ((0, (0, 2)), (1, (4, 6)))
              for v, b in (("sc1", bb[0]), ("sh1", bb[1])) for h in range(2)]
    order += [(f"hT_{g}_{q}", 2 * g + q) for g in range(G) for q in range(2)]
    order += [("u0", 4), ("u1", 5)]
    order += [(f"cq{g}", g) for g in range(G)] + [(f"ckv{g}", 2 + g) for g in range(G)]
    order += [(f"fb{i}", 4 + i) for i in range(4)]
    order += [(f"mod{n}", 6 + n % 2) for n in range(4, 12)]
    order += [("y0", 4), ("y1", 5), ("hlast", 0)]
    order += [("glu0", 6), ("glu1", 7)]
    order += [(f"cqT{g}", g) for g in range(G)] + [(f"ckvT{b}", 2 + b) for b in range(3)]
    nxt = [5]

    def ring(name):
        order.append((name, nxt[0] % 8))
        nxt[0] += 1
    for g in range(G):
        for q in range(2):
            ring(f"q_{g}_{q}")
    for b in range(3):
        ring(f"k{b}")
    for b in range(3):
        ring(f"v{b}")
    for g in range(G):
        for q in range(2):
            ring(f"qT_{g}_{q}")
    for b in range(3):
        for q in range(2):
            ring(f"kT_{b}_{q}")
    for g in range(G):
        for q in range(2 + 2 * g):
            ring(f"s_{g}_{q}")
    for g in range(G):
        for q in range(2 + 2 * g):
            ring(f"pT_{g}_{q}")
        ring(f"at{g}")
    for g in range(G):
        for h in range(2):
            ring(f"bc_g1_{g}_{h}")
    for g in range(G):
        for h in range(2):
            ring(f"mix_{g}_{h}")
    for g in range(G):
        for v in ("sc2", "sh2"):
            for h in range(2):
                ring(f"bc_{v}_{g}_{h}")
        for q in range(2):
            ring(f"h2T_{g}_{q}")
        for n in range(4):
            ring(f"qry_{g}_{n}")
        for q in range(4):
            ring(f"sc_{g}_{q}")
    for g in range(G):
        for h in range(2):
            ring(f"bc_g2_{g}_{h}")
    order += [(f"acc_{g}_{h}", 2 * g + h) for g in range(G) for h in range(2)]
    plan, uses = {}, [0] * 8
    for name, bank in order:
        uses[bank] += 1
        plan[name] = (bank, uses[bank])
    return plan


VEC = {"sh1": 0, "sc1": 1, "g1": 2, "sh2": 3, "sc2": 4, "g2": 5}


def layer(nc, x_prompt, x_sample, c_cols, w_mod, b_mod, norm1, w_in, lam, bmat, cmat, ssm_d, h0,
          w_glu, q_norm, w_uq, kv_norm, w_ukv, w_out, norm2, w_query, keys, u_table, v_table,
          final_norm, cache_ckv, cache_krope, rope_tab, ident_in, sel_in, iota_in,
          y_prompt, y_sample, new_ckv, new_krope, new_ssm):
    plan = bank_plan()
    with ExitStack() as ctx:
        def sb(name, shape, dt=F32):
            return ctx.enter_context(nc.sbuf_tensor(name, shape, dt))

        def sem(name):
            return ctx.enter_context(nc.semaphore(name))

        ring = sb("ring", [P, NSLOT, WSLOT])
        arena = sb("arena", [P, 25600])
        x = sb("x", [P, G, D])
        h = sb("h", [P, G, D])
        hT = sb("hT", [P, KD, G * P])
        mixT = hT
        modrow = sb("modrow", [P, 3, 512])
        brow = sb("brow", [P, 3, 512])
        pad = hT[:, 0:KD // 2, :].rearrange("p k n -> p (k n)").rearrange("p (j r n) -> p j r n", j=4, r=2)
        h_flat = h[:, :, :].rearrange("p g n -> p (g n)")
        uT = h_flat[:, 0:NC * G * P].rearrange("p (c n) -> p c n", c=NC)
        cqn = h_flat[:, 1024:1024 + G * QR].rearrange("p (g n) -> p g n", g=G)
        ckvn = hT[:, KD // 2:KD, :].rearrange("p k n -> p (k n)")[:, 0:3 * KVR].rearrange("p (b n) -> p b n", b=3)
        krope = sb("krope", [P, 3, ROPE])
        ident = sb("ident", [P, P])
        sel = sb("sel", [P, G, P])
        iota = sb("iota", [P, P])
        rope = sb("rope", [P, 2, ROPE])
        ccol = sb("ccol", [P, KD, G])
        scol = sb("scol", [P, KD, G])
        small = sb("small", [P, 768])
        half_neg = sb("half_neg", [P, 4])
        stage = sb("stage", [P, 2 * 2 * BATCH], U32)
        psum = ctx.enter_context(nc.psum_tensor("psum", [P, 8, 512], F32))

        at = [0]

        def part(n):
            at[0] += n
            return small[:, at[0] - n:at[0]]
        ms, rstd = part(2), part(2)
        ms_a, rstd_a = part(4), part(4)
        ms_2, rstd_2 = part(2), part(2)
        ms_f, rstd_f = part(2), part(2)
        dcol = part(NC)
        DT = 2 * TILES
        lam_sb = part(3 * DT)
        lre, lim, ldt = lam_sb[:, 0:DT], lam_sb[:, DT:2 * DT], lam_sb[:, 2 * DT:3 * DT]
        h0_sb = part(2 * DT)
        dtv, rad, turns, kturn, t0, t1 = (part(DT) for _ in range(6))
        are, aim, fre, fim, rden = (part(DT) for _ in range(5))
        init = part(2 * DT)
        hlast = part(2 * DT)
        mx, nb, rs, rr = part(8), part(8), part(8), part(8)
        dots, gel, wts = part(2 * BATCH), part(2 * BATCH), part(2 * BATCH)

        sin_t = arena[:, 0:4096].rearrange("p (a t) -> p a t", a=DT)
        cos_t = arena[:, 4096:8192].rearrange("p (a t) -> p a t", a=DT)
        fbT = arena[:, 8192:10240].rearrange("p (a n) -> p a n", a=16)
        cm = arena[:, 10240:12288].rearrange("p (r a c) -> p r a c", r=2, c=32)
        cneg = arena[:, 24576:25600].rearrange("p (a c) -> p a c", c=32)
        pm = arena[:, 12288:16384].rearrange("p (d k n) -> p d k n", d=2, k=4)
        vm = arena[:, 16384:18432].rearrange("p (d r n) -> p d r n", d=2, r=2)
        gm = arena[:, 18432:20480].rearrange("p (d r n) -> p d r n", d=2, r=2)
        qm = arena[:, 20480:24576].rearrange("p (d k n) -> p d k n", d=2, k=4)
        bm = arena[:, 12288:14336].rearrange("p (r a c) -> p r a c", r=2, c=32)
        fb = arena[:, 14336:16384].rearrange("p (r a c) -> p r a c", r=2, c=32)
        n1b = arena[:, 16384:17408]
        tmpA = arena[:, 17408:18432]
        qnb = arena[:, 18432:18432 + QR]
        kvb = arena[:, 18944:18944 + KVR]
        fbt1 = arena[:, 20480:21504].rearrange("p (a c) -> p a c", c=32)
        fbt2 = arena[:, 21504:22528].rearrange("p (a c) -> p a c", c=32)
        junk1 = arena[:, 22528:23552]
        hlT = arena[0:2 * DT, 22528 + 1024:22528 + 1024 + P]
        yT = arena[:, 0:1024].rearrange("p (c n) -> p c n", c=NC)
        ygT = arena[:, 1024:2048].rearrange("p (c n) -> p c n", c=NC)
        sgT = arena[:, 2048:3072].rearrange("p (c n) -> p c n", c=NC)
        o = [3072]

        def take(n):
            o[0] += n
            return arena[:, o[0] - n:o[0]]
        cqT = take(G * 3 * P).rearrange("p (g k n) -> p g k n", g=G, k=3)
        ckvT = take(3 * 2 * P).rearrange("p (b k n) -> p b k n", b=3, k=2)
        qtok = take(G * HEADS * QK).rearrange("p (g a d) -> p g a d", g=G, a=HEADS)
        ktok = take(3 * HEADS * QK).rearrange("p (b a d) -> p b a d", b=3, a=HEADS)
        vtok = take(3 * 512).rearrange("p (b n) -> p b n", b=3)
        qT = take(G * HEADS * P).rearrange("p (g a n) -> p g a n", g=G, a=HEADS)
        kT = take(HEADS * 3 * P).rearrange("p (a b n) -> p a b n", a=HEADS, b=3)
        rt = take(HEADS * ROPE * 2).rearrange("p (i a d) -> p i a d", i=2, a=HEADS)
        probs = take(HEADS * 256)
        prT = take(HEADS * 2 * P).rearrange("p (a n) -> p a n", n=P)
        g1b = arena[:, 0:2048].rearrange("p (g n) -> p g n", g=G)
        n2b = arena[:, 2048:3072]
        tmpB = arena[:, 3072:4096]
        junk2 = arena[:, 4096:5120]
        qryT = arena[:, 5120:7168].rearrange("p (i n) -> p i n", i=HI)
        keys_sb = arena[:, 7168:9216].rearrange("p (i n) -> p i n", i=HI)
        s_sb = arena[:, 9216:13312].rearrange("p (g i n) -> p g i n", g=G, i=HI)
        s2 = arena[:, 13312:15360].rearrange("p (i n) -> p i n", i=HI)
        cand = arena[:, 15360:17408].rearrange("p (a n) -> p a n", a=PH)
        cand2 = arena[:, 17408:19456].rearrange("p (a n) -> p a n", a=PH)
        hot = arena[:, 0:2048].rearrange("p (a j n) -> p a j n", a=PH, j=TOPK)
        tops = arena[:, 19456:19712].rearrange("p (i n) -> p i n", i=HI)
        topi = arena[:, 19712:19968].bitcast(U32).rearrange("p (i n) -> p i n", i=HI)
        topf = arena[:, 19968:20224].rearrange("p (i n) -> p i n", i=HI)
        best = arena[:, 20224:20352].rearrange("p (a n) -> p a n", a=PH)
        pos = arena[:, 20352:20480].bitcast(U32).rearrange("p (a n) -> p a n", a=PH)
        posa = arena[:, 20480:20608].bitcast(U32)
        posb = arena[:, 20608:20736].bitcast(U32)
        posaf = arena[:, 20736:20864].rearrange("p (a n) -> p a n", a=PH)
        posbf = arena[:, 20864:20992].rearrange("p (a n) -> p a n", a=PH)
        i0 = arena[:, 20992:21120]
        i1 = arena[:, 21120:21248]
        idx = arena[:, 21248:21504].bitcast(U32)
        gate = arena[:, 21504:21760]
        fnb = arena[:, 21760:22784]
        diag = arena[:, 22784:22784 + BATCH * P].rearrange("p (k n) -> p k n", k=BATCH)
        ssum, rsum = arena[:, 23808:23816], arena[:, 23816:23824]
        g2b = arena[:, 5120:7168].rearrange("p (g n) -> p g n", g=G)
        junk3, junk4 = arena[:, 7168:8192], arena[:, 8192:9216]
        out2 = arena[:, 24576:25600]
        zero = arena[:, 23824:24336]
        slots = ring[:, :, :].rearrange("p s (k n) -> p (s k) n", n=D)

        filled = [sem(f"bank{b}_filled") for b in range(8)]
        emptied = [sem(f"bank{b}_emptied") for b in range(8)]
        landed = [sem(f"slot{s}_landed") for s in range(NSLOT)]
        c_in, x_in, s5_in, cst_in, late_in, cache_in = sem("c_in"), sem("x_in"), sem("s5_in"), sem("cst_in"), sem("late_in"), sem("cache_in")
        act_step, dve_step, pool_step = sem("act_step"), sem("dve_step"), sem("pool_step")
        silu_ready = sem("silu_ready")
        sq_ready, rstd_ready = sem("sq_ready"), sem("rstd_ready")
        modrow_ready = sem("modrow_ready")
        h_ready = sem("h_ready")
        dt_ready, lr_ready, r_ready = sem("dt_ready"), sem("lr_ready"), sem("r_ready")
        angle_ready, tab_ready, f_ready, fb_ready = sem("angle_ready"), sem("tab_ready"), sem("f_ready"), sem("fb_ready")
        s5c_ready = sem("s5c_ready")
        latent_ready, krope_ready = sem("latent_ready"), sem("krope_ready")
        bu_ready, bu_used = sem("bu_ready"), sem("bu_used")
        pad_zero, pad_ready, keys_in = sem("pad_zero"), sem("pad_ready"), sem("keys_in")
        prod_ready, v_ready, g_ready, qd_ready, qp_ready, q_used = (
            sem(n) for n in ("prod_ready", "v_ready", "g_ready", "qd_ready", "qp_ready", "q_used"))
        last_ready = sem("last_ready")
        y_ready, yg_ready, sig_ready, ssm_ready = sem("y_ready"), sem("yg_ready"), sem("sig_ready"), sem("ssm_ready")
        q_ready, k_ready, nb_ready, exp_ready, probs_ready = (
            sem(n) for n in ("q_ready", "k_ready", "nb_ready", "exp_ready", "probs_ready"))
        h2_ready, sq2_ready, rstd2_ready = sem("h2_ready"), sem("sq2_ready"), sem("rstd2_ready")
        n2_in, fn_in = sem("n2_in"), sem("fn_in")
        best_ready, gexp_ready, idx_ready, gate_ready = (
            sem(n) for n in ("best_ready", "gexp_ready", "idx_ready", "gate_ready"))
        staged, stepped = sem("staged"), sem("stepped")
        u_landed = [sem(f"u{k}_landed") for k in range(BATCH)]
        v_landed = [sem(f"v{k}_landed") for k in range(BATCH)]
        u_free, gel_ready, wts_ready, diag_ready, v_free, zero_ready = (
            sem(n) for n in ("u_free", "gel_ready", "wts_ready", "diag_ready", "v_free", "zero_ready"))
        sqf_ready, rstdf_ready, y_out_ready = sem("sqf_ready"), sem("rstdf_ready"), sem("y_out_ready")
        stored = sem("stored")

        block = ctx.enter_context(nc.Block())

        def bank(name, *cut):
            return psum[:, plan[name][0], :]

        def wait_filled(eng, name):
            b, n = plan[name]
            eng.wait_ge(filled[b], n)

        def wait_emptied(eng, name):
            b, n = plan[name]
            eng.wait_ge(emptied[b], n)

        def empties(ins, name):
            ins.then_inc(emptied[plan[name][0]], 1)

        def slot_of(name):
            n = LOADS.index(name)
            return n % NSLOT, 16 * (n // NSLOT + 1)

        def weight(name, cols, k=KD):
            return ring[:, slot_of(name)[0], 0:k * cols].rearrange("p (k n) -> p k n", k=k)

        SRC = {f"mod{n}": (w_mod[:, 512 * n:512 * n + 512].rearrange("(k p) n -> p k n", p=P), KD, 512)
               for n in range(12)}
        SRC["in_u"] = (w_in[:, 0:SSM].rearrange("(k p) n -> p k n", p=P), KD, SSM)
        SRC["in_q"] = (w_in[:, SSM:SSM + QR].rearrange("(k p) n -> p k n", p=P), KD, QR)
        SRC["in_kv"] = (w_in[:, SSM + QR:SSM + QR + KVR + ROPE].rearrange("(k p) n -> p k n", p=P), KD, KVR + ROPE)
        SRC["glu"] = (w_glu.rearrange("(k p) n -> p k n", p=P), 4, SSM)
        SRC["uq"] = (w_uq.rearrange("(k p) n -> p k n", p=P), 3, HEADS * QK)
        SRC["ukv"] = (w_ukv.rearrange("w (k p) n -> p (w k) n", p=P), 4, 512)
        for i in range(2):
            SRC[f"out{i}"] = (w_out[:, 512 * i:512 * i + 512].rearrange("(k p) n -> p k n", p=P), KD, 512)
        for i in range(4):
            SRC[f"query{i}"] = (w_query[:, 512 * i:512 * i + 512].rearrange("(k p) n -> p k n", p=P), KD, 512)
        LAST = {f"mod{n}": f"mod{n}" for n in range(12)}
        LAST |= {"in_u": "u1", "in_q": "cq1", "in_kv": "ckv1", "glu": "glu1", "uq": "q_1_1", "ukv": "v2",
                 "out0": "mix_1_0", "out1": "mix_1_1"}
        LAST |= {f"query{n}": f"qry_1_{n}" for n in range(4)}

        @block.sync
        def _(sp):
            def load(n):
                name = LOADS[n]
                src, k, cols = SRC[name]
                if n >= NSLOT:
                    wait_filled(sp, LAST[LOADS[n - NSLOT]])
                sp.dma_start(weight(name, cols, k), src).then_inc(landed[n % NSLOT], 16)

            sp.dma_start(ccol[:, :, :], c_cols).then_inc(c_in, 16)
            sp.dma_start(lam_sb, lam).then_inc(s5_in, 16)
            for n in range(2):
                load(n)
            sp.dma_start(x[:, 0, :], x_prompt).then_inc(x_in, 16)
            sp.dma_start(x[:, 1, :], x_sample).then_inc(x_in, 16)
            sp.dma_start(iota[:, :], iota_in).then_inc(s5_in, 16)
            sp.dma_start(h0_sb, h0).then_inc(s5_in, 16)
            sp.dma_start(bm, bmat).then_inc(s5_in, 16)
            sp.dma_start(brow[:, :, :], b_mod).then_inc(cst_in, 16)
            sp.dma_start(sel[:, :, :], sel_in).then_inc(cst_in, 16)
            sp.dma_start(ident[:, :], ident_in).then_inc(cst_in, 16)
            sp.dma_start(n1b, norm1.to_broadcast([P, D])).then_inc(cst_in, 16)
            for n in range(2, 4):
                load(n)
            sp.dma_start(cm, cmat).then_inc(late_in, 16)
            sp.dma_start(dcol, ssm_d).then_inc(late_in, 16)
            sp.dma_start(qnb, q_norm.to_broadcast([P, QR])).then_inc(late_in, 16)
            sp.dma_start(kvb, kv_norm.to_broadcast([P, KVR])).then_inc(late_in, 16)
            sp.dma_start(rope[:, :, :], rope_tab).then_inc(late_in, 16)
            sp.dma_start(krope[:, 1, :], cache_krope).then_inc(late_in, 16)
            for n in range(4, len(LOADS)):
                load(n)
                if LOADS[n] == "mod6":
                    wait_filled(sp, "ckv1")
                    sp.dma_start(ckvn[:, 1, :], cache_ckv).then_inc(cache_in, 16)
                if LOADS[n] == "out1":
                    wait_filled(sp, "at1")
                    sp.dma_start(n2b, norm2.to_broadcast([P, D])).then_inc(n2_in, 16)
                    sp.dma_start(keys_sb, keys).then_inc(keys_in, 16)
                    sp.dma_start(fnb, final_norm.to_broadcast([P, D])).then_inc(fn_in, 16)
            for g, y in enumerate((y_prompt, y_sample)):
                sp.wait_ge(y_out_ready, g + 1)
                sp.dma_start(y, h[:, g, :]).then_inc(stored, 16)
            sp.wait_ge(stored, 5 * 16)

        @block.tensor
        def _(pe):
            def start(name):
                b, n = plan[name]
                if n > 1:
                    pe.wait_ge(emptied[b], n - 1)
                return psum[:, b, :]

            def finish(ins, name):
                ins.then_inc(filled[plan[name][0]], 1)

            def arrived(name):
                s, n = slot_of(name)
                pe.wait_ge(landed[s], n)

            def mod_chunk(n):
                arrived(f"mod{n}")
                out, w, j = start(f"mod{n}"), weight(f"mod{n}", 512), 32 * (n % 4)
                for k in range(KD):
                    mm = pe.matmul(out[j:j + G, :], scol[:, k, :], w[:, k, :], start=k == 0, stop=k == KD - 1,
                                   tile_position=(0, j))
                finish(mm, f"mod{n}")

            def mod_pair(n):
                outs = []
                for m in (n, n + 1):
                    arrived(f"mod{m}")
                    outs.append((start(f"mod{m}"), weight(f"mod{m}", 512), 32 * (m % 4)))
                for k in range(KD):
                    for i, (out, w, j) in enumerate(outs):
                        mm = pe.matmul(out[j:j + G, :], scol[:, k, :], w[:, k, :], start=k == 0, stop=k == KD - 1,
                                       tile_position=(0, j))
                        if k == KD - 1:
                            finish(mm, f"mod{n + i}")

            def broadcast(v, g):
                for half in range(2):
                    n = 2 * VEC[v] + half
                    name, j = f"bc_{v}_{g}_{half}", 32 * (n % 4)
                    out = start(name)
                    mm = pe.matmul(out, sel[j:j + G, g, :], modrow[j:j + G, n // 4, :], start=True, stop=True)
                    finish(mm, name)

            def transposes(name, sources, rows=P):
                out = start(name)
                for i, src in enumerate(sources):
                    mm = pe.transpose(out[0:rows, P * i:P * i + P], src, ident[:, :])
                finish(mm, name)

            pe.wait_ge(silu_ready, 1)
            for n in range(4):
                mod_chunk(n)
            pe.wait_ge(cst_in, 64)
            pe.wait_ge(modrow_ready, 1)
            for g in range(G):
                broadcast("sc1", g)
                broadcast("sh1", g)
            for g in range(G):
                pe.wait_ge(h_ready, g + 1)
                for q in range(2):
                    transposes(f"hT_{g}_{q}", [h[:, g, P * k:P * k + P] for k in range(4 * q, 4 * q + 4)])
            for g in range(G):
                for q in range(2):
                    wait_emptied(pe, f"hT_{g}_{q}")

            arrived("in_u")
            w = weight("in_u", SSM)
            for c in range(NC):
                out = start(f"u{c // 2}") if c % 2 == 0 else out
                for k in range(KD):
                    mm = pe.matmul(out[:, 256 * (c % 2):256 * (c % 2) + 256], w[:, k, P * c:P * c + P], hT[:, k, :],
                                   start=k == 0, stop=k == KD - 1)
                if c % 2:
                    finish(mm, f"u{c // 2}")
            for name, load, cols in (("cq", "in_q", QR), ("ckv", "in_kv", KVR + ROPE)):
                arrived(load)
                w = weight(load, cols)
                for g in range(G):
                    out = start(f"{name}{g}")
                    for k in range(KD):
                        mm = pe.matmul(out[:, 0:cols], hT[:, k, P * g:P * g + P], w[:, k, :],
                                       start=k == 0, stop=k == KD - 1)
                    finish(mm, f"{name}{g}")

            pe.wait_ge(fb_ready, 1)
            for i in range(4):
                transposes(f"fb{i}", [fb[:, i // 2, 16 * (i % 2) + 4 * q:16 * (i % 2) + 4 * q + 4, :]
                                      .rearrange("p a c -> p (a c)") for q in range(4)])

            for name in ("u0", "u1", "cq0", "cq1", "ckv0", "ckv1"):
                wait_emptied(pe, name)
            for i in range(4):
                wait_emptied(pe, f"fb{i}")
            pe.wait_ge(s5c_ready, 2)

            def tokens(ap, d):
                ap = ap.rearrange("p (g t) -> p g t", g=G)
                return ap[:, :, ::-1] if d else ap

            def s5_in_mm(tp, d):
                if tp:
                    pe.wait_ge(bu_used, 2 * (tp - 1) + d + 1)
                pe.wait_ge(pad_ready, 2 * (2 * tp + d + 1))
                for i in range(2):
                    tile = 2 * tp + i
                    for r in range(2):
                        mm = pe.matmul(psum[:, 2 * d + i, 256 * r:256 * r + 256],
                                       pad[:, tile % 4, r, :], tokens(uT[:, tile // 4, :], d), start=True, stop=True)
                mm.then_inc(bu_ready, 1)

            def s5_out_mm(tp, d):
                pe.wait_ge(qd_ready, 4 * tp + 2 * d + 2)
                pe.wait_ge(qp_ready, 4 * tp + 2 * d + 3)
                if d == 0 and tp in (0, 4):
                    start(f"y{tp // 4}")
                for k in range(4):
                    for i in range(2):
                        tile = 2 * tp + i
                        j, c = 32 * (tile % 4), tile // 4
                        mm = pe.matmul(psum[j:j + 32, 4 + c // 2, 256 * (c % 2):256 * (c % 2) + 256],
                                       (cm[:, 0], cneg, cm[:, 1], cm[:, 1])[k][:, TILES * d + tile, :],
                                       tokens(qm[:, d, k, 256 * i:256 * i + 256], d),
                                       start=d == 0 and k == 0, stop=d == 1 and k == 3, tile_position=(0, j))
                mm.then_inc(q_used, 1)

            pe.sem_inc(q_used, 1)
            for d in range(2):
                s5_in_mm(0, d)
            for tp in range(TILES // 2):
                if tp % 2 == 0:
                    mod_pair(4 + tp)
                for d in range(2):
                    if tp + 1 < TILES // 2:
                        s5_in_mm(tp + 1, d)
                for d in range(2):
                    s5_out_mm(tp, d)
                if tp % 4 == 3:
                    pe.wait_ge(q_used, 2 * tp + 3)
                    pe.sem_inc(filled[4 + tp // 4], 1)
            pe.wait_ge(last_ready, 2 * TILES + 1)
            b, n = plan["hlast"]
            pe.wait_ge(bu_used, TILES)
            pe.transpose(psum[0:2 * DT, b, 0:P], hlast, ident[:, :]).then_inc(filled[b], 1)

            pe.wait_ge(yg_ready, 2)
            arrived("glu")
            w = weight("glu", SSM, 4)
            for c in range(NC):
                out = start(f"glu{c // 2}") if c % 2 == 0 else out
                for k in range(4):
                    mm = pe.matmul(out[:, 256 * (c % 2):256 * (c % 2) + 256], w[:, k, P * c:P * c + P], ygT[:, k, :],
                                   start=k == 0, stop=k == 3)
                if c % 2:
                    finish(mm, f"glu{c // 2}")

            for g in range(G):
                transposes(f"cqT{g}", [cqn[:, g, P * k:P * k + P] for k in range(3)])
            pe.wait_ge(cache_in, 16)
            for b in range(3):
                transposes(f"ckvT{b}", [ckvn[:, b, P * k:P * k + P] for k in range(2)])
            for g in range(G):
                wait_emptied(pe, f"cqT{g}")
            arrived("uq")
            w = weight("uq", HEADS * QK, 3)
            for g in range(G):
                for q in range(2):
                    out = start(f"q_{g}_{q}")
                    for k in range(3):
                        mm = pe.matmul(out[:, 0:384], cqT[:, g, k, :], w[:, k, 384 * q:384 * q + 384],
                                       start=k == 0, stop=k == 2)
                    finish(mm, f"q_{g}_{q}")
            for b in range(3):
                wait_emptied(pe, f"ckvT{b}")
            arrived("ukv")
            w = weight("ukv", 512, 4)
            for m, name in enumerate("kv"):
                for b in range(3):
                    out = start(f"{name}{b}")
                    for k in range(2):
                        mm = pe.matmul(out, ckvT[:, b, k, :], w[:, 2 * m + k, :], start=k == 0, stop=k == 1)
                    finish(mm, f"{name}{b}")
            for g in range(G):
                pe.wait_ge(q_ready, g + 1)
                for q in range(2):
                    transposes(f"qT_{g}_{q}", [qtok[:, g, a, :] for a in range(4 * q, 4 * q + 4)], QK)
            pe.wait_ge(k_ready, 3)
            for b in range(3):
                wait_emptied(pe, f"k{b}")
                for q in range(2):
                    transposes(f"kT_{b}_{q}", [ktok[:, b, a, :] for a in range(4 * q, 4 * q + 4)], QK)
            for b in range(3):
                for q in range(2):
                    wait_emptied(pe, f"kT_{b}_{q}")
            for g in range(G):
                per, nb_, b0 = (4, 1, 0) if g == 0 else (2, 2, 1)
                wait_emptied(pe, f"qT_{g}_0")
                wait_emptied(pe, f"qT_{g}_1")
                for q in range(2 + 2 * g):
                    out = start(f"s_{g}_{q}")
                    for a in range(per):
                        mm = pe.matmul(out[:, nb_ * P * a:nb_ * P * (a + 1)], qT[0:QK, g, per * q + a, :],
                                       kT[0:QK, per * q + a, b0:b0 + nb_, :], start=True, stop=True)
                    finish(mm, f"s_{g}_{q}")
            for b in range(3):
                wait_emptied(pe, f"v{b}")
            for g in range(G):
                pe.wait_ge(probs_ready, g + 1)
                for q in range(2 + 2 * g):
                    transposes(f"pT_{g}_{q}", [probs[:, P * i:P * i + P] for i in range(4 * q, 4 * q + 4)])
                for q in range(2 + 2 * g):
                    wait_emptied(pe, f"pT_{g}_{q}")
                out = start(f"at{g}")
                for a in range(HEADS):
                    r = 64 * (a % 2)
                    for b in range(1 + g):
                        mm = pe.matmul(out[r:r + VD, P * (a // 2):P * (a // 2) + P],
                                       vtok[:, g + b, VD * a:VD * a + VD], prT[:, (1 + g) * a + b, :],
                                       start=b == 0, stop=b == g, tile_position=(0, r))
                finish(mm, f"at{g}")

            pe.wait_ge(modrow_ready, 2)
            for g in range(G):
                broadcast("g1", g)
            for g in range(G):
                wait_emptied(pe, f"at{g}")
            pe.wait_ge(ssm_ready, 2)
            for g in range(G):
                for half in range(2):
                    arrived(f"out{half}")
                    w, out = weight(f"out{half}", 512), start(f"mix_{g}_{half}")
                    for k in range(KD):
                        mm = pe.matmul(out, mixT[:, k, P * g:P * g + P], w[:, k, :], start=k == 0, stop=k == KD - 1)
                    finish(mm, f"mix_{g}_{half}")
            for g in range(G):
                broadcast("sc2", g)
                broadcast("sh2", g)
                pe.wait_ge(h2_ready, g + 1)
                for q in range(2):
                    transposes(f"h2T_{g}_{q}", [h[:, g, P * k:P * k + P] for k in range(4 * q, 4 * q + 4)])
                for q in range(2):
                    wait_emptied(pe, f"h2T_{g}_{q}")
                for n in range(4):
                    arrived(f"query{n}")
                    w, out = weight(f"query{n}", 512), start(f"qry_{g}_{n}")
                    for i in range(4):
                        for k in range(KD):
                            mm = pe.matmul(out[:, P * i:P * i + P], w[:, k, P * i:P * i + P], hT[:, k, P * g:P * g + P],
                                           start=k == 0, stop=k == KD - 1)
                    finish(mm, f"qry_{g}_{n}")
                for n in range(4):
                    wait_emptied(pe, f"qry_{g}_{n}")
                pe.wait_ge(keys_in, 16)
                for q in range(4):
                    out = start(f"sc_{g}_{q}")
                    for i in range(4):
                        mm = pe.matmul(out[:, P * i:P * i + P], qryT[:, 4 * q + i, :], keys_sb[:, 4 * q + i, :],
                                       start=True, stop=True)
                    finish(mm, f"sc_{g}_{q}")
            for g in range(G):
                broadcast("g2", g)

            pe.wait_ge(zero_ready, 1)
            for g in range(G):
                for half in range(2):
                    pe.matmul(start(f"acc_{g}_{half}"), zero[:, 0:P], zero[:, :], start=True, stop=False)
                with pe.Fori(0, NB) as i:
                    for k in range(BATCH):
                        it = NB * g + i
                        pe.wait_ge(diag_ready, BATCH * it + (k + 2))
                        pe.wait_ge(v_landed[k], 16 * (it + 1))
                        for half in range(2):
                            mm = pe.matmul(bank(f"acc_{g}_{half}"), diag[:, k, :],
                                           slots[:, BATCH + k, 512 * half:512 * half + 512], start=False, stop=False)
                        mm.then_inc(v_free, 1)
                for half in range(2):
                    finish(pe.matmul(bank(f"acc_{g}_{half}"), zero[:, 0:P], zero[:, :], start=False, stop=True),
                           f"acc_{g}_{half}")

        @block.scalar
        def _(act):
            n = [0]

            def step(ins):
                n[0] += 1
                ins.then_inc(act_step, 1)
                act.wait_ge(act_step, n[0])

            def evacuate(dst, src, name, last=True):
                wait_filled(act, name)
                ins = act.copy(dst, src)
                if last:
                    empties(ins, name)

            act.wait_ge(c_in, 16)
            act.activation(scol[:, :, :], ccol[:, :, :], ACT.Silu).then_inc(silu_ready, 1)
            act.wait_ge(s5_in, 64)
            act.activation(dtv, ldt, ACT.Exp).then_inc(dt_ready, 1)
            act.wait_ge(lr_ready, 1)
            act.activation(rad, t0, ACT.Exp).then_inc(r_ready, 1)
            act.wait_ge(angle_ready, 1)
            act.activation(arena[:, 0:8192], arena[:, 0:8192], ACT.Sin, scale=6.283185).then_inc(tab_ready, 1)

            def soft_exp(g):
                act.wait_ge(best_ready, g + 1)
                act.activation(gate[:, PICKS * g:PICKS * g + PICKS], gate[:, PICKS * g:PICKS * g + PICKS],
                               ACT.Exp).then_inc(gexp_ready, 1)

            def mod_evac(m):
                j = 32 * (m % 4)
                evacuate(modrow[j:j + G, m // 4, :], bank(f"mod{m}")[j:j + G, :], f"mod{m}")
            act.wait_ge(pool_step, 1)
            for m in range(4):
                mod_evac(m)
            for g in range(G):
                for q in range(2):
                    evacuate(hT[:, 4 * q:4 * q + 4, P * g:P * g + P], bank(f"hT_{g}_{q}").rearrange("p (k n) -> p k n", k=4),
                             f"hT_{g}_{q}")
            for i in range(2):
                evacuate(uT[:, 2 * i:2 * i + 2, :], bank(f"u{i}"), f"u{i}")
            for g in range(G):
                wait_filled(act, f"cq{g}")
                act.activation(junk1[:, 0:QR], bank(f"cq{g}")[:, 0:QR], ACT.Square,
                               accum_out=ms_a[:, g:g + 1]).then_inc(sq_ready, 1)
                act.wait_ge(sq_ready, 3 + 2 * g)
                wait_filled(act, f"ckv{g}")
                act.activation(junk1[:, 0:KVR], bank(f"ckv{g}")[:, 0:KVR], ACT.Square,
                               accum_out=ms_a[:, 2 + g:3 + g]).then_inc(sq_ready, 1)
                act.wait_ge(sq_ready, 4 + 2 * g)
            for i in range(4):
                evacuate(fbT[:, 4 * i:4 * i + 4, :], bank(f"fb{i}"), f"fb{i}")
            for i in range(4):
                wait_emptied(act, f"fb{i}")
            act.wait_ge(pad_zero, 1)
            for tp in range(TILES // 2):
                for d in range(2):
                    if d:
                        act.wait_ge(bu_ready, 2 * tp + 1)
                    elif tp >= 2:
                        act.wait_ge(bu_ready, 2 * (tp - 1))
                    for i in range(2):
                        tile = 2 * tp + i
                        j = tile % 4
                        act.copy(pad[32 * j:32 * j + 32, j, :, :],
                                 fbT[32 * j:32 * j + 32, d * 4 + tile // 4:16:8, :]).then_inc(pad_ready, 1)
                if tp == 1:
                    act.wait_ge(krope_ready, 1)
                    act.wait_ge(latent_ready, 2)
                    act.dma_start(new_ckv, ckvn[:, 0, :]).then_inc(stored, 16)
                    act.dma_start(new_krope, krope[:, 0, :]).then_inc(stored, 16)
                if tp % 2:
                    for m in (3 + tp, 4 + tp):
                        mod_evac(m)
            evacuate(hlT, bank("hlast")[0:2 * DT, 0:P], "hlast")
            wait_emptied(act, "hlast")
            act.dma_start(new_ssm, hlT).then_inc(stored, 16)
            for i in range(2):
                act.wait_ge(y_ready, i + 1)
                act.activation(ygT[:, 2 * i:2 * i + 2, :], yT[:, 2 * i:2 * i + 2, :], ACT.Gelu_apprx_tanh).then_inc(yg_ready, 1)
            for i in range(2):
                wait_filled(act, f"glu{i}")
                empties(act.activation(sgT[:, 2 * i:2 * i + 2, :], bank(f"glu{i}"), ACT.Sigmoid), f"glu{i}")
            for g in range(G):
                evacuate(cqT[:, g, :, :], bank(f"cqT{g}")[:, 0:QR].rearrange("p (k n) -> p k n", k=3), f"cqT{g}")
            for b in range(3):
                evacuate(ckvT[:, b, :, :], bank(f"ckvT{b}")[:, 0:KVR].rearrange("p (k n) -> p k n", k=2), f"ckvT{b}")
            for b in range(3):
                evacuate(ktok[:, b, :, 0:NOPE], bank(f"k{b}").rearrange("p (a d) -> p a d", a=HEADS), f"k{b}")
            for b in range(3):
                evacuate(vtok[:, b, :], bank(f"v{b}"), f"v{b}")
            for b in range(3):
                for q in range(2):
                    evacuate(kT[0:QK, 4 * q:4 * q + 4, b, :],
                             bank(f"kT_{b}_{q}")[0:QK, :].rearrange("p (a n) -> p a n", a=4), f"kT_{b}_{q}")
            for g in range(G):
                per, nb_ = (4, 1) if g == 0 else (2, 2)
                act.wait_ge(nb_ready, g + 1)
                if g:
                    wait_filled(act, "pT_0_1")
                for a in range(HEADS):
                    w = nb_ * P
                    ins = act.activation(probs[:, w * a:w * a + w],
                                         bank(f"s_{g}_{a // per}")[:, w * (a % per):w * (a % per) + w], ACT.Exp,
                                         bias=nb[:, a:a + 1], scale=SCALE, accum_out=rs[:, a:a + 1])
                    if a % per == per - 1:
                        empties(ins, f"s_{g}_{a // per}")
                    else:
                        step(ins)
                for q in range(2 + 2 * g):
                    evacuate(prT[:, 4 * q:4 * q + 4, :], bank(f"pT_{g}_{q}").rearrange("p (a n) -> p a n", a=4),
                             f"pT_{g}_{q}")
                act.wait_ge(stored, 3 * 16)
                evacuate(mixT[:, 4:8, P * g:P * g + P], bank(f"at{g}").rearrange("p (a n) -> p a n", a=4), f"at{g}")
            for g in range(G):
                for half in range(2):
                    evacuate(g1b[:, g, 512 * half:512 * half + 512], bank(f"bc_g1_{g}_{half}"), f"bc_g1_{g}_{half}")
            for g in range(G):
                for q in range(2):
                    evacuate(hT[:, 4 * q:4 * q + 4, P * g:P * g + P],
                             bank(f"h2T_{g}_{q}").rearrange("p (k n) -> p k n", k=4), f"h2T_{g}_{q}")
                for n in range(4):
                    evacuate(qryT[:, 4 * n:4 * n + 4, :], bank(f"qry_{g}_{n}"), f"qry_{g}_{n}")
                for q in range(4):
                    evacuate(s_sb[:, g, 4 * q:4 * q + 4, :], bank(f"sc_{g}_{q}"), f"sc_{g}_{q}")
            soft_exp(0)
            for g in range(G):
                for half in range(2):
                    evacuate(g2b[:, g, 512 * half:512 * half + 512], bank(f"bc_g2_{g}_{half}"), f"bc_g2_{g}_{half}")
            act.sem_inc(gel_ready, 1)
            act.sem_inc(diag_ready, 1)
            for g in range(G):
                if g:
                    soft_exp(1)
                with act.Fori(0, NB) as i:
                    it = NB * g + i
                    act.wait_ge(u_free, BATCH * (it + 2))
                    act.activation(gel[:, 0:BATCH], dots[:, 0:BATCH], ACT.Gelu_apprx_tanh).then_inc(gel_ready, 1)
                    act.wait_ge(wts_ready, it + 1)
                    for k in range(BATCH):
                        act.wait_ge(v_free, BATCH * it + (k + 1))
                        act.activation(diag[:, k, :], ident[:, :], ACT.Copy, scale=wts[:, k:k + 1]).then_inc(diag_ready, 1)

        @block.gpsimd
        def _(pool):
            n = [0]

            def step(ins):
                n[0] += 1
                ins.then_inc(pool_step, 1)
                pool.wait_ge(pool_step, n[0])

            step(pool.memset(modrow[:, :, :], 0.0))
            step(pool.memset(half_neg[:, :], -0.5))

            def inverse_root(out, src, width, ready, signal):
                pool.wait_ge(*ready)
                for lo, hi, w in width:
                    step(pool.tensor_scalar(src[:, lo:hi], src[:, lo:hi], 1.0 / w, EPS, ALU.mult, ALU.add))
                pool.tensor_tensor(out, src, half_neg[:, 0:src.shape[1]], ALU.pow).then_inc(signal, 1)

            inverse_root(rstd, ms, [(0, 2, D)], (sq_ready, 2), rstd_ready)
            pool.wait_ge(f_ready, 1)

            def spread(v):
                return v.unsqueeze(2).to_broadcast([P, DT, 32])
            for r, (first, second, op) in enumerate(((fre, fim, ALU.subtract), (fim, fre, ALU.add))):
                step(pool.tensor_tensor(fbt1, bm[:, 0, :, :], spread(first), ALU.mult))
                step(pool.tensor_tensor(fbt2, bm[:, 1, :, :], spread(second), ALU.mult))
                ins = pool.tensor_tensor(fb[:, r, :, :], fbt1, fbt2, op)
                if r == 0:
                    step(ins)
                else:
                    ins.then_inc(fb_ready, 1)
            pool.wait_ge(late_in, 6 * 16)
            for dst, src in ((cneg, cm[:, 0, :, :]), (cm[:, 1, :, :], cm[:, 1, :, :])):
                pool.tensor_scalar(dst, src, -1.0, 0.0, ALU.mult, ALU.add).then_inc(s5c_ready, 1)
            inverse_root(rstd_a, ms_a, [(0, 2, QR), (2, 4, KVR)], (sq_ready, 6), rstd_ready)
            wait_filled(pool, "ckv1")
            pool.memset(pad, 0.0).then_inc(pad_zero, 1)

            for counted in (v_ready, qp_ready, last_ready):
                pool.sem_inc(counted, 1)
            with pool.Fori(0, TILES // 2) as tp:
                for d in range(2):
                    pool.wait_ge(prod_ready, 8 * tp + (4 * d + 2))
                    pool.tensor_tensor(vm[:, d, 0, :], pm[:, d, 0, :], pm[:, d, 1, :], ALU.add).then_inc(v_ready, 1)
                    pool.wait_ge(prod_ready, 8 * tp + (4 * d + 4))
                    pool.tensor_tensor(vm[:, d, 1, :], pm[:, d, 2, :], pm[:, d, 3, :], ALU.subtract).then_inc(v_ready, 1)
                for d in range(2):
                    pool.wait_ge(g_ready, 16 * tp + (8 * d + 8))
                    pool.wait_ge(q_used, 2 * tp + 1)
                    for k, tab, r in ((2, sin_t, 0), (3, cos_t, 1)):
                        ins = pool.tensor_tensor(
                            qm[:, d, k, :].rearrange("p (i g t) -> p i g t", i=2, g=G),
                            gm[:, d, r, :].rearrange("p (i g t) -> p i g t", i=2, g=G),
                            tab[:, bass.ds(TILES * d + 2 * tp, 2), :].unsqueeze(2).to_broadcast([P, 2, G, P]), ALU.mult)
                        ins.then_inc(qp_ready, 1)
                    pool.wait_ge(qd_ready, 4 * tp + (2 * d + 2))
                    pool.wait_ge(qp_ready, 4 * tp + (2 * d + 3))
                    for r, op in ((0, ALU.subtract), (1, ALU.add)):
                        a_, b_ = (qm[:, d, 2 * r + e, :].rearrange("p (i n) -> p i n", i=2)[:, :, P - 1] for e in range(2))
                        pool.tensor_tensor(hlast[:, bass.ds(TILES * (2 * d + r) + 2 * tp, 2)], a_, b_,
                                           op).then_inc(last_ready, 1)

            wait_emptied(pool, "hlast")
            for b in range(3):
                pool.tensor_copy(ktok[:, b, :, NOPE:QK], krope[:, b:b + 1, :].to_broadcast([P, HEADS, ROPE])).then_inc(k_ready, 1)

            for g in range(G):
                inverse_root(rstd_2[:, g:g + 1], ms_2[:, g:g + 1], [(0, 1, D)], (sq2_ready, g + 1), rstd2_ready)

            for name in ("qry_1_3",):
                wait_filled(pool, name)
            for g in range(G):
                pool.wait_ge(idx_ready, g + 1)
                with pool.Fori(0, NB // 2) as i:
                    for half in range(2):
                        it = NB * g + 2 * i + half
                        st = stage[:, BATCH * half:BATCH * half + BATCH]
                        pool.tensor_copy(st, idx[:, bass.ds(PICKS * g + 2 * BATCH * i + BATCH * half, BATCH)]).then_inc(staged, 1)
                        pool.wait_ge(staged, it + 1)
                        pool.sem_inc(stepped, 1)
                        for table, used, sems, base in ((u_table, u_free, u_landed, 0), (v_table, v_free, v_landed, BATCH)):
                            for k in range(BATCH):
                                pool.wait_ge(used, BATCH * it + (k + 1))
                                pool.sem_inc(stepped, 1)
                                pool.indirect_dma_start(slots[:, base + k, :], None, table,
                                                        bass.IndirectOffsetOnAxis(ap=st[:, k:k + 1], axis=0)).then_inc(sems[k], 16)
            for g in range(G):
                inverse_root(rstd_f[:, g:g + 1], ms_f[:, g:g + 1], [(0, 1, D)], (sqf_ready, g + 1), rstdf_ready)

        @block.vector
        def _(dve):
            n = [0]

            def step(ins):
                n[0] += 1
                ins.then_inc(dve_step, 1)
                dve.wait_ge(dve_step, n[0])

            def tt(out, a, b, op):
                step(dve.tensor_tensor(out, a, b, op))

            dve.wait_ge(x_in, 32)
            for g in range(G):
                dve.tensor_tensor_reduce(out=junk1, in0=x[:, g, :], in1=x[:, g, :], scale=1.0, scalar=0.0,
                                         op0=ALU.mult, op1=ALU.add, accum_out=ms[:, g:g + 1]).then_inc(sq_ready, 1)
                dve.wait_ge(sq_ready, g + 1)
            dve.wait_ge(dt_ready, 1)
            dve.wait_ge(s5_in, 64)
            dve.tensor_tensor(t0, lre, dtv, ALU.mult).then_inc(lr_ready, 1)
            tt(turns, lim, dtv, ALU.mult)
            step(dve.tensor_scalar(kturn, turns, INV_2PI, MAGIC, ALU.mult, ALU.add))
            step(dve.tensor_scalar(kturn, kturn, MAGIC, None, ALU.subtract))
            step(dve.scalar_tensor_tensor(turns, kturn, -C1, turns, ALU.mult, ALU.add))
            step(dve.scalar_tensor_tensor(turns, kturn, -C2, turns, ALU.mult, ALU.add))
            step(dve.tensor_scalar(turns, turns, INV_2PI, None, ALU.mult))
            tt(sin_t, turns.unsqueeze(2).to_broadcast([P, DT, P]), iota[:, :].unsqueeze(1).to_broadcast([P, DT, P]), ALU.mult)
            step(dve.tensor_scalar(cos_t, sin_t, MAGIC, MAGIC, ALU.add, ALU.subtract))
            tt(sin_t, sin_t, cos_t, ALU.subtract)
            step(dve.tensor_scalar(cos_t, sin_t, 0.25, None, ALU.is_gt))
            dve.scalar_tensor_tensor(cos_t, sin_t, 0.25, cos_t, ALU.add, ALU.subtract).then_inc(angle_ready, 1)
            dve.wait_ge(angle_ready, 1)
            dve.wait_ge(cst_in, 64)
            for m in range(4):
                wait_emptied(dve, f"mod{m}")
            dve.wait_ge(pool_step, 1)
            dve.tensor_tensor(modrow[:, 0, :], modrow[:, 0, :], brow[:, 0, :], ALU.add).then_inc(modrow_ready, 1)

            def modulated(g, scale_, shift, norm, tmp, root, signal):
                for half in range(2):
                    cut = slice(512 * half, 512 * half + 512)
                    name = f"bc_{scale_}_{g}_{half}"
                    wait_filled(dve, name)
                    ins = dve.scalar_tensor_tensor(tmp[:, cut], bank(name), 1.0, norm[:, cut], ALU.add, ALU.mult)
                    empties(ins, name)
                    wait_emptied(dve, name)
                step(dve.scalar_tensor_tensor(h[:, g, :], x[:, g, :], root[:, g:g + 1], tmp, ALU.mult, ALU.mult))
                for half in range(2):
                    cut = slice(512 * half, 512 * half + 512)
                    name = f"bc_{shift}_{g}_{half}"
                    wait_filled(dve, name)
                    empties(dve.tensor_tensor(h[:, g, cut], h[:, g, cut], bank(name), ALU.add), name)
                    wait_emptied(dve, name)
                dve.sem_inc(signal, 1)

            dve.wait_ge(rstd_ready, 1)
            for g in range(G):
                modulated(g, "sc1", "sh1", n1b, tmpA, rstd, h_ready)

            dve.wait_ge(tab_ready, 1)
            dve.wait_ge(r_ready, 1)
            c1, s1 = cos_t[:, :, 1], sin_t[:, :, 1]
            tt(are, rad, c1, ALU.mult)
            tt(aim, rad, s1, ALU.mult)
            tt(t0, lre, lre, ALU.mult)
            tt(t1, lim, lim, ALU.mult)
            tt(t0, t0, t1, ALU.add)
            step(dve.reciprocal(rden, t0))
            step(dve.tensor_scalar(are, are, -1.0, None, ALU.add))
            tt(t0, are, lre, ALU.mult)
            tt(t1, aim, lim, ALU.mult)
            tt(t0, t0, t1, ALU.add)
            tt(fre, t0, rden, ALU.mult)
            tt(t0, aim, lre, ALU.mult)
            tt(t1, are, lim, ALU.mult)
            tt(t0, t0, t1, ALU.subtract)
            dve.tensor_tensor(fim, t0, rden, ALU.mult).then_inc(f_ready, 1)
            dve.wait_ge(f_ready, 1)
            hr, hi = h0_sb[:, 0:DT], h0_sb[:, DT:2 * DT]
            for r, (a_, b_, op) in enumerate(((c1, s1, ALU.subtract), (s1, c1, ALU.add))):
                tt(t0, hr, a_, ALU.mult)
                tt(t1, hi, b_, ALU.mult)
                tt(init[:, DT * r:DT * r + DT], t0, t1, op)

            def rotary(dst, src, tmp, heads, tail):
                def quarters(ap):
                    return ap.rearrange("p a (r s f) -> p a r s f", r=2, s=2)
                cs = rope[:, 0:1, :].to_broadcast([P, heads, ROPE])
                sn = rope[:, 1:2, :].to_broadcast([P, heads, ROPE])
                step(dve.tensor_tensor(tmp[:, 0], src, cs, ALU.mult))
                for r in range(2):
                    for s_ in range(2):
                        at_, of = 16 * r + 8 * s_, 16 * r + 8 * (1 - s_)
                        step(dve.tensor_tensor(tmp[:, 1, :, at_:at_ + 8], src[:, :, of:of + 8], sn[:, :, at_:at_ + 8], ALU.mult))
                tail(dve.tensor_tensor(dst, tmp[:, 0], tmp[:, 1], ALU.add))

            dve.wait_ge(rstd_ready, 2)
            dve.wait_ge(late_in, 6 * 16)
            wait_filled(dve, "ckv1")
            for g in range(G):
                wait_filled(dve, f"cq{g}")
                dve.scalar_tensor_tensor(cqn[:, g, :], bank(f"cq{g}")[:, 0:QR], rstd_a[:, g:g + 1], qnb,
                                         ALU.mult, ALU.mult).then_inc(emptied[plan[f"cq{g}"][0]], 1)
                wait_filled(dve, f"ckv{g}")
                step(dve.tensor_copy(krope[:, 2 * g, :], bank(f"ckv{g}")[:, KVR:KVR + ROPE]))
                dve.scalar_tensor_tensor(ckvn[:, 2 * g, :], bank(f"ckv{g}")[:, 0:KVR], rstd_a[:, 2 + g:3 + g], kvb,
                                         ALU.mult, ALU.mult).then_inc(emptied[plan[f"ckv{g}"][0]], 1)
                wait_emptied(dve, f"ckv{g}")
                dve.sem_inc(latent_ready, 1)
            dve.sem_inc(latent_ready, 1)
            krt = junk1[:, 512:576].rearrange("p (i a d) -> p i a d", i=2, a=1)
            rotary(krope[:, 2:3, :], krope[:, 2:3, :], krt, 1, lambda ins: ins.then_inc(krope_ready, 1))
            dve.wait_ge(krope_ready, 1)
            for m in ("cq0", "cq1"):
                wait_emptied(dve, m)

            def view(ap):
                return ap.rearrange("p (i g t) -> p i g t", i=2, g=G)
            dve.wait_ge(fb_ready, 1)
            with dve.Fori(0, TILES // 2) as tp:
                def table(tab, d):
                    return tab[:, bass.ds(TILES * d + 2 * tp, 2), :].unsqueeze(2).to_broadcast([P, 2, G, P])
                for d in range(2):
                    dve.wait_ge(bu_ready, 2 * tp + (d + 1))
                    dve.wait_ge(v_ready, 4 * tp + 1)
                    bu = psum[:, 2 * d:2 * d + 2, :].rearrange("p i (r g t) -> p r i g t", r=2, g=G)
                    for k, (r, tab) in enumerate(((0, cos_t), (1, sin_t), (1, cos_t), (0, sin_t))):
                        ins = dve.tensor_tensor(view(pm[:, d, k, :]), bu[:, r], table(tab, d), ALU.mult)
                        ins.then_inc(prod_ready, 1)
                    dve.wait_ge(prod_ready, 8 * tp + (4 * d + 4))
                    dve.sem_inc(bu_used, 1)
                for d in range(2):
                    dve.wait_ge(qp_ready, 4 * tp + 1)
                    for r in range(2):
                        dve.wait_ge(v_ready, 4 * tp + (2 * d + r + 2))
                        for i in range(2):
                            for g in range(G):
                                cut = slice(256 * i + P * g, 256 * i + P * g + P)
                                start_ = init[:, bass.ds(DT * r + TILES * d + 2 * tp + i, 1)] if g else 0.0
                                dve.tensor_tensor_scan(
                                    gm[:, d, r, cut], rad[:, bass.ds(TILES * d + 2 * tp + i, 1)].to_broadcast([P, P]),
                                    vm[:, d, r, cut], start_, ALU.mult, ALU.add).then_inc(g_ready, 1)
                    dve.wait_ge(g_ready, 16 * tp + (8 * d + 8))
                    dve.wait_ge(q_used, 2 * tp + 1)
                    dve.wait_ge(last_ready, 4 * tp + 1)
                    for k, (r, tab) in enumerate(((0, cos_t), (1, sin_t))):
                        dve.tensor_tensor(view(qm[:, d, k, :]), view(gm[:, d, r, :]), table(tab, d),
                                          ALU.mult).then_inc(qd_ready, 1)

            for i in range(2):
                wait_filled(dve, f"y{i}")
                for c in (2 * i, 2 * i + 1):
                    ins = dve.scalar_tensor_tensor(yT[:, c, :], uT[:, c, :], dcol[:, c:c + 1],
                                                   bank(f"y{i}")[:, 256 * (c % 2):256 * (c % 2) + 256], ALU.mult, ALU.add)
                    if c % 2:
                        empties(ins, f"y{i}")
                    else:
                        step(ins)
                wait_emptied(dve, f"y{i}")
                dve.sem_inc(y_ready, 1)
            for m in range(4, 12):
                wait_emptied(dve, f"mod{m}")
            dve.tensor_tensor(modrow[:, 1:3, :], modrow[:, 1:3, :], brow[:, 1:3, :], ALU.add).then_inc(modrow_ready, 1)
            for i in range(2):
                wait_emptied(dve, f"glu{i}")
                dve.tensor_tensor(mixT[:, 2 * i:2 * i + 2, :], ygT[:, 2 * i:2 * i + 2, :], sgT[:, 2 * i:2 * i + 2, :],
                                  ALU.mult).then_inc(ssm_ready, 1)

            for g in range(G):
                for q in range(2):
                    name = f"q_{g}_{q}"
                    wait_filled(dve, name)
                    src = bank(name)[:, 0:384].rearrange("p (a d) -> p a d", a=4)
                    dst = qtok[:, g, 4 * q:4 * q + 4, :]
                    if g == 0:
                        empties(dve.tensor_copy(dst, src), name)
                    else:
                        step(dve.tensor_copy(dst[:, :, 0:NOPE], src[:, :, 0:NOPE]))
                        rotary(dst[:, :, NOPE:QK], src[:, :, NOPE:QK], rt[:, :, 4 * q:4 * q + 4, :], 4,
                               lambda ins: empties(ins, name))
                    wait_emptied(dve, name)
                dve.sem_inc(q_ready, 1)
            for g in range(G):
                for q in range(2):
                    wait_filled(dve, f"qT_{g}_{q}")
                    empties(dve.tensor_copy(qT[0:QK, g, 4 * q:4 * q + 4, :],
                                            bank(f"qT_{g}_{q}")[0:QK, :].rearrange("p (a n) -> p a n", a=4)), f"qT_{g}_{q}")
            for g in range(G):
                per = 4 if g == 0 else 2
                for q in range(2 + 2 * g):
                    wait_filled(dve, f"s_{g}_{q}")
                    step(dve.tensor_reduce(mx[:, per * q:per * q + per],
                                           bank(f"s_{g}_{q}").rearrange("p (a n) -> p a n", a=per), AX.X, ALU.max))
                dve.tensor_scalar(nb, mx, -SCALE, None, ALU.mult).then_inc(nb_ready, 1)
                for q in range(2 + 2 * g):
                    wait_emptied(dve, f"s_{g}_{q}")
                step(dve.reciprocal(rr, rs))
                pv = probs[:, 0:HEADS * P * (1 + g)].rearrange("p (a n) -> p a n", a=HEADS)
                dve.tensor_tensor(pv, pv, rr.unsqueeze(2).to_broadcast([P, HEADS, P * (1 + g)]),
                                  ALU.mult).then_inc(probs_ready, 1)

            wait_filled(dve, "at1")
            dve.memset(zero, 0.0).then_inc(zero_ready, 1)
            for g in range(G):
                for half in range(2):
                    wait_emptied(dve, f"bc_g1_{g}_{half}")
            for g in range(G):
                for half in range(2):
                    name, cut = f"mix_{g}_{half}", slice(512 * half, 512 * half + 512)
                    wait_filled(dve, name)
                    empties(dve.tensor_tensor(tmpB[:, cut], bank(name), g1b[:, g, cut], ALU.mult), name)
                    wait_emptied(dve, name)
                    tt(x[:, g, cut], x[:, g, cut], tmpB[:, cut], ALU.add)
                dve.tensor_tensor_reduce(out=junk2, in0=x[:, g, :], in1=x[:, g, :], scale=1.0, scalar=0.0,
                                         op0=ALU.mult, op1=ALU.add, accum_out=ms_2[:, g:g + 1]).then_inc(sq2_ready, 1)
                dve.wait_ge(rstd2_ready, g + 1)
                dve.wait_ge(n2_in, 16)
                modulated(g, "sc2", "sh2", n2b, tmpB, rstd_2, h2_ready)

            def top16(values, spare, out_v, out_i, rows):
                for first in (0, 8):
                    src = values if first == 0 else spare
                    for r in range(rows):
                        last = dve.max(out_v[:, r, first:first + 8], src[:, r, :])
                    step(last)
                    yield
                    for r in range(rows):
                        last = dve.max_index(out_i[:, r, first:first + 8], out_v[:, r, first:first + 8], src[:, r, :])
                        if first == 0:
                            last = dve.match_replace(spare[:, r, :], out_v[:, r, 0:8], values[:, r, :], LOW)
                        if r == rows // 2 - 1:
                            yield
                    step(last)
                    yield

            def gates(g):
                return gate[:, PICKS * g:PICKS * g + PICKS].rearrange("p (a n) -> p a n", a=PH)

            def experts(g):
                for q in range(4):
                    wait_emptied(dve, f"sc_{g}_{q}")
                yield from top16(s_sb[:, g], s2, tops, topi, HI)
                step(dve.tensor_copy(topf, topi))
                pair = tops.rearrange("p (a r) n -> p a r n", r=2)
                pairf = topf.rearrange("p (a r) n -> p a r n", r=2)
                wide = [P, PH, TOPK, TOPK]
                tt(cand.rearrange("p a (i j) -> p a i j", i=TOPK), pair[:, :, 0, :].unsqueeze(3).to_broadcast(wide),
                   pair[:, :, 1, :].unsqueeze(2).to_broadcast(wide), ALU.add)
                yield
                yield from top16(cand, cand2, best, pos, PH)
                dve.tensor_tensor(gates(g), best, best[:, :, 0:1].to_broadcast([P, PH, TOPK]),
                                  ALU.subtract).then_inc(best_ready, 1)
                flat = pos.rearrange("p a n -> p (a n)")
                step(dve.tensor_scalar(posa, flat, 4, None, ALU.logical_shift_right))
                step(dve.tensor_scalar(posb, flat, 15, None, ALU.bitwise_and))
                step(dve.tensor_copy(posaf.rearrange("p a n -> p (a n)"), posa))
                step(dve.tensor_copy(posbf.rearrange("p a n -> p (a n)"), posb))
                yield
                for r, (at_, out) in enumerate(((posaf, i0), (posbf, i1))):
                    tt(hot, at_.unsqueeze(3).to_broadcast(wide),
                       iota[:, 0:TOPK].unsqueeze(1).unsqueeze(1).to_broadcast(wide), ALU.is_equal)
                    yield
                    tt(hot, hot, pairf[:, :, r, :].unsqueeze(2).to_broadcast(wide), ALU.mult)
                    yield
                    step(dve.tensor_reduce(out.rearrange("p (a n) -> p a n", a=PH), hot, AX.X, ALU.add))
                    yield
                dve.scalar_tensor_tensor(idx[:, PICKS * g:PICKS * g + PICKS], i0, float(NKEYS), i1,
                                         ALU.mult, ALU.add).then_inc(idx_ready, 1)

            def normalise_gates(g):
                dve.wait_ge(gexp_ready, g + 1)
                step(dve.tensor_reduce(ssum, gates(g), AX.X, ALU.add))
                step(dve.reciprocal(rsum, ssum))
                tt(gates(g), gates(g), rsum.unsqueeze(2).to_broadcast([P, PH, TOPK]), ALU.mult)

            def weigh(g, first, last):
                with dve.Fori(first, last) as i:
                    it = NB * g + i
                    for k in range(BATCH):
                        if k == 0:
                            dve.wait_ge(gel_ready, it + 1)
                        dve.wait_ge(u_landed[k], 16 * (it + 1))
                        dve.wait_ge(u_free, BATCH * (it + 1) + (k - 1))
                        dve.tensor_tensor_reduce(out=junk4 if k % 2 else junk3, in0=slots[:, k, :], in1=h[:, g, :], scale=1.0, scalar=0.0,
                                                 op0=ALU.mult, op1=ALU.add, accum_out=dots[:, k:k + 1]).then_inc(u_free, 1)
                    dve.wait_ge(gel_ready, it + 2)
                    dve.wait_ge(diag_ready, BATCH * it + 1)
                    dve.tensor_tensor(wts[:, 0:BATCH], gel[:, 0:BATCH],
                                      gate[:, bass.ds(PICKS * g + BATCH * i, BATCH)], ALU.mult).then_inc(wts_ready, 1)

            def add_experts(g):
                for half in range(2):
                    name, cut = f"acc_{g}_{half}", slice(512 * half, 512 * half + 512)
                    wait_filled(dve, name)
                    wait_emptied(dve, f"bc_g2_{g}_{half}")
                    empties(dve.tensor_tensor(out2[:, cut], bank(name), g2b[:, g, cut], ALU.mult), name)
                    wait_emptied(dve, name)
                    tt(x[:, g, cut], x[:, g, cut], out2[:, cut], ALU.add)
                dve.tensor_tensor_reduce(out=out2, in0=x[:, g, :], in1=x[:, g, :], scale=1.0, scalar=0.0,
                                         op0=ALU.mult, op1=ALU.add, accum_out=ms_f[:, g:g + 1]).then_inc(sqf_ready, 1)
                dve.wait_ge(sqf_ready, g + 1)

            def finish_group(g):
                dve.wait_ge(rstdf_ready, g + 1)
                dve.wait_ge(fn_in, 16)
                dve.scalar_tensor_tensor(h[:, g, :], x[:, g, :], rstd_f[:, g:g + 1], fnb,
                                         ALU.mult, ALU.mult).then_inc(y_out_ready, 1)

            for _ in experts(0):
                pass
            normalise_gates(0)
            wait_filled(dve, "sc_1_3")
            dve.sem_inc(u_free, BATCH)
            dve.sem_inc(v_free, BATCH)
            rest = experts(1)
            weigh(0, 0, 1)
            for i in range(1, NB, 2):
                for _ in range(2):
                    next(rest, None)
                weigh(0, i, min(i + 2, NB))
            for _ in rest:
                pass
            normalise_gates(1)
            weigh(1, 0, 2)
            add_experts(0)
            weigh(1, 2, NB)
            add_experts(1)
            for g in range(G):
                finish_group(g)


def rope_tables(tokens=P, grid=64, base=10000.0):
    half = ROPE // 2
    inv = (1.0 / (np.float32(base) ** (np.arange(0, half, 2, dtype=np.float32) / np.float32(half)))).astype(np.float32)
    row = (np.arange(tokens) // grid).astype(np.float32)[:, None] * inv
    col = (np.arange(tokens) % grid).astype(np.float32)[:, None] * inv
    ang = np.concatenate([row, row, col, col], axis=-1)
    sign = np.where((np.arange(ROPE) // (ROPE // 4)) % 2 == 0, -1.0, 1.0)
    return np.stack([np.cos(ang), np.sin(ang) * sign], axis=1).astype(np.float32)


def by_state(a):
    a = np.asarray(a)
    lead = a.shape[:-2]
    a = a.reshape(lead + (TILES, 2, SN))
    n = len(lead)
    return np.ascontiguousarray(a.transpose((n + 1, n + 2) + tuple(range(n + 1)))).reshape(P, -1)


def block_diagonal(a):
    a = np.asarray(a).reshape(2, TILES, 2, SN, SP_)
    out = np.zeros((2, SN, 2, TILES, 2, SP_), a.dtype)
    for e in range(2):
        out[e, :, :, :, e, :] = a[:, :, e].transpose(2, 0, 1, 3)
    return out.reshape(P, 2 * TILES, 32)


def kernel(**inputs):
    import concourse.bacc as bacc
    from concourse.bass_utils import run_bass_kernel_spmd as run

    a = {k: np.asarray(v) for k, v in inputs.items()}
    brow = np.zeros((P, 3, 512), np.float32)
    for n in range(12):
        for g in range(G):
            brow[32 * (n % 4) + g, n // 4] = a["b_mod"][0, 512 * n:512 * n + 512]
    sel = np.zeros((P, G, P), np.float32)
    for j in range(0, P, 32):
        for g in range(G):
            sel[j + g, g] = 1.0
    ldt = np.repeat(a["ssm_log_dt"][0][:, :, None], SN, axis=2)
    arrays = {
        "x_prompt": a["x_prompt"][0], "x_sample": a["x_sample"][0],
        "c_cols": np.stack([a["c_ctx"], a["c"][0]], axis=1).reshape(KD, P, G).transpose(1, 0, 2),
        "w_mod": a["w_mod"][0], "b_mod": brow, "norm1": a["norm1"], "w_in": a["w_in"][0],
        "lam": np.concatenate([by_state(v) for v in (a["ssm_lam_re"][0], a["ssm_lam_im"][0], ldt)], axis=1),
        "bmat": np.stack([block_diagonal(a[k][0]) for k in ("ssm_b_re", "ssm_b_im")], axis=1),
        "cmat": np.stack([block_diagonal(a[k][0].transpose(0, 1, 3, 2)) for k in ("ssm_c_re", "ssm_c_im")], axis=1),
        "ssm_d": a["ssm_d"][0].reshape(NC, P).T,
        "h0": by_state(a["state_ssm"][0, 0].transpose(1, 0, 2, 3)),
        "w_glu": a["w_glu"][0], "q_norm": a["q_norm"], "w_uq": a["w_uq"][0], "kv_norm": a["kv_norm"],
        "w_ukv": np.stack([a["w_uk"][0], a["w_uv"][0]]), "w_out": a["w_out"][0], "norm2": a["norm2"],
        "w_query": a["w_query"][0],
        "keys": a["sub_keys"][0].reshape(HI, NKEYS, P).transpose(2, 0, 1),
        "u_table": a["u_table"][0], "v_table": a["v_table"][0], "final_norm": a["final_norm"][None],
        "cache_ckv": a["cache_ckv"][0, 0], "cache_krope": a["cache_krope"][0, 0],
        "rope_tab": rope_tables(), "ident_in": np.eye(P, dtype=np.float32), "sel_in": sel,
        "iota_in": np.tile(np.arange(P, dtype=np.float32), (P, 1)),
    }
    arrays = {k: np.ascontiguousarray(v) for k, v in arrays.items()}
    outs = {"y_prompt": (P, D), "y_sample": (P, D), "new_ckv": (P, KVR), "new_krope": (P, ROPE), "new_ssm": (2 * 2 * TILES, P)}
    nc = bacc.Bacc("TRN2", target_bir_lowering=False, num_devices=1)
    aps = {k: nc.dram_tensor(k, v.shape, F32, kind="ExternalInput").ap() for k, v in arrays.items()}
    aps |= {k: nc.dram_tensor(k, s, F32, kind="ExternalOutput").ap() for k, s in outs.items()}
    layer(nc, **aps)
    r = run(nc, [arrays], core_ids=[0]).results[0]
    return (r["y_prompt"].reshape(1, P, D), r["y_sample"].reshape(1, P, D), r["new_ckv"].reshape(1, 1, P, KVR),
            r["new_krope"].reshape(1, 1, P, ROPE), r["new_ssm"].reshape(1, 1, 2, 2, SG, SN))
```

```python
import math
from contextlib import ExitStack

import numpy as np

import concourse.bass as bass
from concourse import mybir

F32 = mybir.dt.float32
U32 = mybir.dt.uint32
ALU = mybir.AluOpType
ACT = mybir.ActivationFunctionType
AX = mybir.AxisListType

P = 128
G = 2
D = 1024
KD = D // P
EPS = 1e-6
SSM = 512
SG, SN, SP_ = 32, 64, 16
TILES = SG * SN // P
NC = SSM // P
QR, KVR, ROPE, NOPE, VD = 384, 256, 32, 64, 64
HEADS = 8
QK = NOPE + ROPE
SCALE = QK ** -0.5
PH, TOPK, NKEYS = 8, 16, 128
HI = PH * 2
PICKS = PH * TOPK
BATCH = 8
NB = PICKS // BATCH
UNITS = 8
UP = PICKS * G // UNITS
WSLOT = KD * 512
NSLOT = 4
MAGIC = 12582912.0
INV_2PI = 1.0 / (2.0 * math.pi)
C1 = 6.28125
C2 = 2.0 * math.pi - C1
LOW = -3.0e38

LOADS = ([f"mod{n}" for n in range(4)] + ["in_u", "in_q", "in_kv"] + [f"mod{n}" for n in range(4, 12)]
         + ["uq", "glu", "ukv", "out0", "out1"] + [f"query{n}" for n in range(4)])


def bank_plan():
    order = [(f"mod{n}", 6 + n % 2) for n in range(4)]
    order += [(f"bc_{v}_{g}_{h}", b + h) for g, bb in ((0, (0, 2)), (1, (4, 6)))
              for v, b in (("sc1", bb[0]), ("sh1", bb[1])) for h in range(2)]
    order += [(f"hT_{g}_{q}", 2 * g + q) for g in range(G) for q in range(2)]
    order += [("u0", 4)] + [(f"fb{i}", i) for i in range(4)] + [("u1", 5)]
    order += [("cq0", 6), ("cq1", 7), ("kv", 5)]
    order += [(f"mod{n}", 6 + n % 2) for n in range(4, 10)]
    order += [(f"cqT{g}", 6 + g) for g in range(G)]
    order += [(f"mod{n}", 6 + n % 2) for n in range(10, 12)]
    order += [(f"ckvT{b}", 6 + b % 2) for b in range(3)]
    order += [("y0", 4), ("y1", 5), ("hlast", 7)]
    order += [(f"q_{g}_{q}", 2 * g + q) for g in range(G) for q in range(2)]
    order += [("glu0", 4), ("glu1", 5)]
    nxt = [6]

    def ring(name):
        order.append((name, nxt[0] % 8))
        nxt[0] += 1
    for b in range(3):
        ring(f"k{b}")
    for b in range(3):
        ring(f"v{b}")
    for g in range(G):
        for q in range(2):
            ring(f"qT_{g}_{q}")
    for b in range(3):
        for q in range(2):
            ring(f"kT_{b}_{q}")
    for g in range(G):
        for q in range(2 + 2 * g):
            ring(f"s_{g}_{q}")
    for q in range(2):
        ring(f"pT_0_{q}")
    ring("at0")
    for h in range(2):
        ring(f"mix_0_{h}")
    for q in range(4):
        ring(f"pT_1_{q}")
    ring("at1")
    for h in range(2):
        ring(f"mix_1_{h}")
    for q in range(2):
        ring(f"h2T_0_{q}")
    ring("qry_0_0")
    ring("sc_0_0")
    for q in range(2):
        ring(f"h2T_1_{q}")
    ring("qry_1_0")
    ring("sc_1_0")
    for n in range(1, 3):
        for g in range(G):
            ring(f"qry_{g}_{n}")
        for g in range(G):
            ring(f"sc_{g}_{n}")
    order += [(f"acc_0_{h}", h) for h in range(2)]
    order += [(f"{v}_{g}_3", b + g) for v, b in (("qry", 4), ("sc", 6)) for g in range(G)]
    order += [(f"acc_1_{h}", 2 + h) for h in range(2)]
    plan, uses = {}, [0] * 8
    for name, bank in order:
        uses[bank] += 1
        plan[name] = (bank, uses[bank])
    return plan


VEC = {"sh1": 0, "sc1": 1, "g1": 2, "sh2": 3, "sc2": 4, "g2": 5}


def layer(nc, x_prompt, x_sample, c_cols, w_mod, b_mod, norm1, w_in, lam, bmat, cmat, ssm_d, h0,
          w_glu, q_norm, w_uq, kv_norm, w_ukv, w_out, norm2, w_query, keys, u_table, v_table,
          final_norm, cache_ckv, cache_krope, rope_tab, ident_in, iota_in,
          y_prompt, y_sample, new_ckv, new_krope, new_ssm):
    plan = bank_plan()
    with ExitStack() as ctx:
        def sb(name, shape, dt=F32):
            return ctx.enter_context(nc.sbuf_tensor(name, shape, dt))

        def sem(name):
            return ctx.enter_context(nc.semaphore(name))

        ring = sb("ring", [P, NSLOT, WSLOT])
        arena = sb("arena", [P, 25600])
        x = sb("x", [P, G, D])
        h = sb("h", [P, G, D])
        hT = sb("hT", [P, KD, G * P])
        mixT = hT
        modrow = sb("modrow", [P, 3, 512])
        brow = sb("brow", [P, 3, 512])
        pads3 = sb("pads3", [P, 3, 2, P])
        h_flat = h[:, :, :].rearrange("p g n -> p (g n)")
        uT = h_flat[:, 0:NC * G * P].rearrange("p (c n) -> p c n", c=NC)
        cqn = h_flat[:, 1024:1024 + G * QR].rearrange("p (g n) -> p g n", g=G)
        pads = [h_flat[:, 1792:2048].rearrange("p (r n) -> p r n", r=2)] + [pads3[:, j] for j in range(3)]
        ckvn = hT[:, KD // 2:KD, :].rearrange("p k n -> p (k n)")[:, 0:3 * KVR].rearrange("p (b n) -> p b n", b=3)
        krope = sb("krope", [P, 3, ROPE])
        ident = sb("ident", [P, P])
        iota = sb("iota", [P, P])
        rope = sb("rope", [P, 2, ROPE])
        ccol = sb("ccol", [P, KD, G])
        scol = sb("scol", [P, KD, G])
        small = sb("small", [P, 720])
        half_neg = sb("half_neg", [P, 4])
        stage = sb("stage", [P, 2 * 2 * BATCH], U32)
        psum = ctx.enter_context(nc.psum_tensor("psum", [P, 8, 512], F32))

        at = [0]

        def part(n):
            at[0] += n
            return small[:, at[0] - n:at[0]]
        ms, rstd = part(2), part(2)
        ms_a, rstd_a = part(4), part(4)
        ms_2, rstd_2 = part(2), part(2)
        ms_f, rstd_f = part(2), part(2)
        dcol = part(NC)
        DT = 2 * TILES
        lam_sb = part(3 * DT)
        lre, lim, ldt = lam_sb[:, 0:DT], lam_sb[:, DT:2 * DT], lam_sb[:, 2 * DT:3 * DT]
        h0_sb = part(2 * DT)
        dtv, rad, turns, kturn, t0, t1 = (part(DT) for _ in range(6))
        are, aim, fre, fim, rden = (part(DT) for _ in range(5))
        init = part(2 * DT)
        hlast = part(2 * DT)
        mx, nb, rs, rr = part(8), part(8), part(8), part(8)
        dots, gel, wts = part(BATCH), part(BATCH), part(BATCH)

        sin_t = arena[:, 0:4096].rearrange("p (a t) -> p a t", a=DT)
        cos_t = arena[:, 4096:8192].rearrange("p (a t) -> p a t", a=DT)
        fbT = arena[:, 8192:10240].rearrange("p (a n) -> p a n", a=16)
        cm = arena[:, 10240:12288].rearrange("p (r a c) -> p r a c", r=2, c=32)
        cneg = arena[:, 24576:25600].rearrange("p (a c) -> p a c", c=32)
        pm = arena[:, 12288:16384].rearrange("p (d k n) -> p d k n", d=2, k=4)
        vm = arena[:, 16384:18432].rearrange("p (d r n) -> p d r n", d=2, r=2)
        gm = arena[:, 18432:20480].rearrange("p (d r n) -> p d r n", d=2, r=2)
        qm = arena[:, 20480:24576].rearrange("p (d k n) -> p d k n", d=2, k=4)
        bm = arena[:, 12288:14336].rearrange("p (r a c) -> p r a c", r=2, c=32)
        fb = arena[:, 14336:16384].rearrange("p (r a c) -> p r a c", r=2, c=32)
        n1b = arena[:, 16384:17408]
        tmpA = arena[:, 17408:18432]
        behind = ring[:, LOADS.index("in_kv") % NSLOT, KD * (KVR + ROPE):WSLOT]
        qnb, kvb, junk5 = behind[:, 0:QR], behind[:, QR:QR + KVR], behind[:, 640:640 + QR]
        krt = behind[:, 1024:1088].rearrange("p (i a d) -> p i a d", i=2, a=1)
        fbt1 = arena[:, 20480:21504].rearrange("p (a c) -> p a c", c=32)
        fbt2 = arena[:, 21504:22528].rearrange("p (a c) -> p a c", c=32)
        junk1 = arena[:, 22528:23552]
        one_step = arena[:, 24448:24448 + 2 * DT].rearrange("p (c a) -> p c a", c=2)
        hlT = arena[0:2 * DT, 23824:23824 + P]
        yT = arena[:, 0:1024].rearrange("p (c n) -> p c n", c=NC)
        ygT = arena[:, 1024:2048].rearrange("p (c n) -> p c n", c=NC)
        sgT = arena[:, 2048:3072].rearrange("p (c n) -> p c n", c=NC)
        hT_flat = hT[:, :, :].rearrange("p k n -> p (k n)")
        cqT = hT_flat[:, 0:G * 3 * P].rearrange("p (g k n) -> p g k n", g=G, k=3)
        ckvT = [ap.rearrange("p (k n) -> p k n", k=2)
                for ap in (arena[:, 3072:3328], hT_flat[:, 1792:2048], arena[:, 3328:3584])]
        o = [4608]

        def take(n):
            o[0] += n
            return arena[:, o[0] - n:o[0]]
        qtok = take(G * HEADS * QK).rearrange("p (g a d) -> p g a d", g=G, a=HEADS)
        ktok = take(3 * HEADS * QK).rearrange("p (b a d) -> p b a d", b=3, a=HEADS)
        vtok = take(3 * 512).rearrange("p (b n) -> p b n", b=3)
        qT = take(G * HEADS * P).rearrange("p (g a n) -> p g a n", g=G, a=HEADS)
        kT = take(HEADS * 3 * P).rearrange("p (a b n) -> p a b n", a=HEADS, b=3)
        rt = take(HEADS * ROPE * 2).rearrange("p (i a d) -> p i a d", i=2, a=HEADS)
        probs = take(HEADS * 256)
        prT = take(HEADS * 2 * P).rearrange("p (a n) -> p a n", n=P)
        g1b = arena[:, 0:2048].rearrange("p (g n) -> p g n", g=G)
        n2b = arena[:, 2048:3072]
        tmpB = arena[:, 3072:4096]
        sc2b = arena[:, 19712:21760].rearrange("p (g n) -> p g n", g=G)
        sh2b = arena[:, 21760:23808].rearrange("p (g n) -> p g n", g=G)
        junk2 = arena[:, 4096:5120]
        qryT = arena[:, 5120:7168].rearrange("p (b i n) -> p b i n", b=4, i=4)
        keys_sb = arena[:, 7168:9216].rearrange("p (i n) -> p i n", i=HI)
        s_sb = arena[:, 9216:13312]
        s2 = arena[:, 13312:13824].rearrange("p (i n) -> p i n", i=4)
        cand = arena[:, 13824:14336].rearrange("p (a n) -> p a n", a=2)
        cand2 = arena[:, 14336:14848].rearrange("p (a n) -> p a n", a=2)
        hot = arena[:, 14848:15360].rearrange("p (a j n) -> p a j n", a=2, j=TOPK)
        o[0] = 19456
        tops = take(64).rearrange("p (i n) -> p i n", i=4)
        topi = take(64).bitcast(U32).rearrange("p (i n) -> p i n", i=4)
        topf = take(64).rearrange("p (i n) -> p i n", i=4)
        best = take(UP).rearrange("p (a n) -> p a n", a=2)
        pos = take(UP).bitcast(U32).rearrange("p (a n) -> p a n", a=2)
        posa, posb = take(UP).bitcast(U32), take(UP).bitcast(U32)
        posaf, posbf = (take(UP).rearrange("p (a n) -> p a n", a=2) for _ in range(2))
        i0, i1 = take(UP), take(UP)
        ssum, rsum = take(2), take(2)
        idx = arena[:, 19968:20224].bitcast(U32)
        gate = arena[:, 20224:20480]
        junk3, junk4 = arena[:, 18432:19456], arena[:, 20480:21504]
        fnb = arena[:, 21760:22784]
        diag = arena[:, 22784:22784 + BATCH * P].rearrange("p (k n) -> p k n", k=BATCH)
        out2 = arena[:, 24576:25600]
        g2b = arena[:, 5120:7168].rearrange("p (g n) -> p g n", g=G)
        u_rows = [arena[:, a:a + D] for a in (0, 1024, 2048, 3072, 4096, 15360, 16384, 17408)]
        v_rows = [ring[:, k // 4, D * (k % 4):D * (k % 4) + D] for k in range(BATCH)]

        filled = [sem(f"bank{b}_filled") for b in range(8)]
        emptied = [sem(f"bank{b}_emptied") for b in range(8)]
        landed = [sem(f"slot{s}_landed") for s in range(NSLOT)]
        c_in, x_in, s5_in, b_in, cst_in, late_in, cache_in = sem("c_in"), sem("x_in"), sem("s5_in"), sem("b_in"), sem("cst_in"), sem("late_in"), sem("cache_in")
        act_step, dve_step, pool_step = sem("act_step"), sem("dve_step"), sem("pool_step")
        silu_ready = sem("silu_ready")
        sq_ready, rstd_ready = sem("sq_ready"), sem("rstd_ready")
        modrow_ready = sem("modrow_ready")
        h_ready = sem("h_ready")
        dt_ready, lr_ready, r_ready = sem("dt_ready"), sem("lr_ready"), sem("r_ready")
        first_ready, angle_ready, tab_ready, f_ready, fb_ready = sem("first_ready"), sem("angle_ready"), sem("tab_ready"), sem("f_ready"), sem("fb_ready")
        s5c_ready = sem("s5c_ready")
        latent_ready, krope_ready = sem("latent_ready"), sem("krope_ready")
        bu_ready, bu_used = sem("bu_ready"), sem("bu_used")
        norm_in, pad_zero, pad_ready, keys_in = sem("norm_in"), sem("pad_zero"), sem("pad_ready"), sem("keys_in")
        prod_ready, v_ready, g_ready, qd_ready, qp_ready, q_used = (
            sem(n) for n in ("prod_ready", "v_ready", "g_ready", "qd_ready", "qp_ready", "q_used"))
        last_ready = sem("last_ready")
        y_ready, yg_ready, ssm_ready = sem("y_ready"), sem("yg_ready"), sem("ssm_ready")
        q_ready, k_ready, nb_ready, probs_ready = (
            sem(n) for n in ("q_ready", "k_ready", "nb_ready", "probs_ready"))
        h2_ready, sq2_ready, rstd2_ready = sem("h2_ready"), sem("sq2_ready"), sem("rstd2_ready")
        n1_in, n2_in, fn_in = sem("n1_in"), sem("n2_in"), sem("fn_in")
        rows_in = {v: sem(f"{v}_in") for v in ("g1", "sc2", "sh2", "g2")}
        best_ready, gexp_ready, idx_ready = (
            sem(n) for n in ("best_ready", "gexp_ready", "idx_ready"))
        scores_ready = sem("scores_ready")
        staged, stepped = sem("staged"), sem("stepped")
        u_landed = [sem(f"u{k}_landed") for k in range(BATCH)]
        v_landed = [sem(f"v{k}_landed") for k in range(BATCH)]
        u_free, gel_ready, wts_ready, diag_ready, v_free = (
            sem(n) for n in ("u_free", "gel_ready", "wts_ready", "diag_ready", "v_free"))
        sqf_ready, rstdf_ready, y_out_ready = sem("sqf_ready"), sem("rstdf_ready"), sem("y_out_ready")
        stored = sem("stored")

        block = ctx.enter_context(nc.Block())

        def bank(name, *cut):
            return psum[:, plan[name][0], :]

        def wait_filled(eng, name):
            b, n = plan[name]
            eng.wait_ge(filled[b], n)

        def wait_emptied(eng, name):
            b, n = plan[name]
            eng.wait_ge(emptied[b], n)

        def empties(ins, name):
            ins.then_inc(emptied[plan[name][0]], 1)

        def slot_of(name):
            n = LOADS.index(name)
            return n % NSLOT, 16 * (n // NSLOT + 1)

        def weight(name, cols, k=KD):
            return ring[:, slot_of(name)[0], 0:k * cols].rearrange("p (k n) -> p k n", k=k)

        SRC = {f"mod{n}": (w_mod[:, 512 * n:512 * n + 512].rearrange("(k p) n -> p k n", p=P), KD, 512)
               for n in range(12)}
        SRC["in_u"] = (w_in[:, 0:SSM].rearrange("(k p) n -> p k n", p=P), KD, SSM)
        SRC["in_q"] = (w_in[:, SSM:SSM + QR].rearrange("(k p) n -> p k n", p=P), KD, QR)
        SRC["in_kv"] = (w_in[:, SSM + QR:SSM + QR + KVR + ROPE].rearrange("(k p) n -> p k n", p=P), KD, KVR + ROPE)
        SRC["glu"] = (w_glu.rearrange("(k p) n -> p k n", p=P), 4, SSM)
        SRC["uq"] = (w_uq.rearrange("(k p) n -> p k n", p=P), 3, HEADS * QK)
        SRC["ukv"] = (w_ukv.rearrange("w (k p) n -> p (w k) n", p=P), 4, 512)
        for i in range(2):
            SRC[f"out{i}"] = (w_out[:, 512 * i:512 * i + 512].rearrange("(k p) n -> p k n", p=P), KD, 512)
        for i in range(4):
            SRC[f"query{i}"] = (w_query[:, 512 * i:512 * i + 512].rearrange("(k p) n -> p k n", p=P), KD, 512)
        LAST = {f"mod{n}": f"mod{n}" for n in range(12)}
        LAST |= {"in_u": "u1", "in_q": "cq1", "in_kv": "kv", "glu": "glu1", "uq": "q_1_1", "ukv": "v2",
                 "out0": "mix_1_0", "out1": "mix_1_1"}
        LAST |= {f"query{n}": f"qry_1_{n}" for n in range(4)}

        @block.sync
        def _(sp):
            def spread_rows(v, out):
                for g in range(G):
                    for half in range(2):
                        n = 2 * VEC[v] + half
                        row = 32 * (n % 4) + g
                        sp.dma_start(out[:, g, 512 * half:512 * half + 512],
                                     modrow[row:row + 1, n // 4, :].unsqueeze(1).to_broadcast([1, P, 512])).then_inc(rows_in[v], 16)

            def load(n):
                name = LOADS[n]
                src, k, cols = SRC[name]
                if n >= NSLOT:
                    wait_filled(sp, LAST[LOADS[n - NSLOT]])
                sp.dma_start(weight(name, cols, k), src).then_inc(landed[n % NSLOT], 16)

            sp.dma_start(ccol[:, :, :], c_cols).then_inc(c_in, 16)
            sp.dma_start(lam_sb, lam).then_inc(s5_in, 16)
            sp.dma_start(iota[:, :], iota_in).then_inc(s5_in, 16)
            load(0)
            sp.dma_start(ident[:, :], ident_in).then_inc(cst_in, 16)
            sp.wait_ge(pool_step, 1)
            for j in range(4):
                sp.dma_start(brow[32 * j:32 * j + G, :, :],
                             b_mod.rearrange("(k j) n -> j k n", j=4)[j:j + 1].to_broadcast([G, 3, 512])).then_inc(cst_in, 16)
            for n in range(1, 4):
                load(n)
            sp.dma_start(x[:, 0, :], x_prompt).then_inc(x_in, 16)
            sp.dma_start(x[:, 1, :], x_sample).then_inc(x_in, 16)
            sp.dma_start(n1b, norm1.to_broadcast([P, D])).then_inc(n1_in, 16)
            sp.dma_start(h0_sb, h0).then_inc(b_in, 16)
            sp.dma_start(bm, bmat).then_inc(b_in, 16)
            load(4)
            sp.dma_start(cm, cmat).then_inc(late_in, 16)
            sp.dma_start(dcol, ssm_d).then_inc(late_in, 16)
            sp.dma_start(rope[:, :, :], rope_tab).then_inc(late_in, 16)
            sp.dma_start(krope[:, 1, :], cache_krope).then_inc(late_in, 16)
            for n in range(5, len(LOADS)):
                if LOADS[n] == "mod7":
                    sp.wait_ge(latent_ready, 2)
                load(n)
                if LOADS[n] == "in_kv":
                    sp.dma_start(qnb, q_norm.to_broadcast([P, QR])).then_inc(norm_in, 16)
                    sp.dma_start(kvb, kv_norm.to_broadcast([P, KVR])).then_inc(norm_in, 16)
                if LOADS[n] == "mod6":
                    wait_filled(sp, "kv")
                    sp.dma_start(ckvn[:, 1, :], cache_ckv).then_inc(cache_in, 16)
                if LOADS[n] == "out0":
                    sp.wait_ge(modrow_ready, 2)
                    sp.wait_ge(last_ready, 2 * TILES + 1)
                    spread_rows("sc2", sc2b)
                    spread_rows("sh2", sh2b)
                    sp.wait_ge(ssm_ready, 2)
                    sp.dma_start(n2b, norm2.to_broadcast([P, D])).then_inc(n2_in, 16)
                    spread_rows("g1", g1b)
                if LOADS[n] == "query1":
                    wait_filled(sp, "at1")
                    sp.dma_start(keys_sb, keys).then_inc(keys_in, 16)
            sp.wait_ge(h2_ready, 2)
            sp.dma_start(fnb, final_norm.to_broadcast([P, D])).then_inc(fn_in, 16)
            for g in range(G):
                wait_filled(sp, f"sc_{g}_3")
            spread_rows("g2", g2b)
            for g, y in enumerate((y_prompt, y_sample)):
                sp.wait_ge(y_out_ready, g + 1)
                sp.dma_start(y, h[:, g, :]).then_inc(stored, 16)
            sp.wait_ge(stored, 5 * 16)

        @block.tensor
        def _(pe):
            def start(name):
                b, n = plan[name]
                if n > 1:
                    pe.wait_ge(emptied[b], n - 1)
                return psum[:, b, :]

            def finish(ins, name):
                ins.then_inc(filled[plan[name][0]], 1)

            def arrived(name):
                s, n = slot_of(name)
                pe.wait_ge(landed[s], n)

            def mod_chunk(n):
                arrived(f"mod{n}")
                out, w, j = start(f"mod{n}"), weight(f"mod{n}", 512), 32 * (n % 4)
                for k in range(KD):
                    mm = pe.matmul(out[j:j + G, :], scol[:, k, :], w[:, k, :], start=k == 0, stop=k == KD - 1,
                                   tile_position=(0, j))
                finish(mm, f"mod{n}")

            def mod_pair(n):
                outs = []
                for m in (n, n + 1):
                    arrived(f"mod{m}")
                    outs.append((start(f"mod{m}"), weight(f"mod{m}", 512), 32 * (m % 4)))
                for k in range(KD):
                    for i, (out, w, j) in enumerate(outs):
                        mm = pe.matmul(out[j:j + G, :], scol[:, k, :], w[:, k, :], start=k == 0, stop=k == KD - 1,
                                       tile_position=(0, j))
                        if k == KD - 1:
                            finish(mm, f"mod{n + i}")

            def broadcast(v, g):
                for half in range(2):
                    n = 2 * VEC[v] + half
                    name, j = f"bc_{v}_{g}_{half}", 32 * (n % 4)
                    out = start(name)
                    mm = pe.matmul(out, ident[:, j + g:j + g + 1].to_broadcast([P, P]), modrow[:, n // 4, :], start=True, stop=True)
                    finish(mm, name)

            def transposes(name, sources, rows=P):
                out = start(name)
                for i, src in enumerate(sources):
                    mm = pe.transpose(out[0:rows, P * i:P * i + P], src, ident[:, :])
                finish(mm, name)

            pe.wait_ge(silu_ready, 1)
            for n in range(4):
                mod_chunk(n)
            pe.wait_ge(cst_in, 80)
            pe.wait_ge(modrow_ready, 1)
            for g in range(G):
                broadcast("sc1", g)
                broadcast("sh1", g)
            for g in range(G):
                pe.wait_ge(h_ready, g + 1)
                for q in range(2):
                    transposes(f"hT_{g}_{q}", [h[:, g, P * k:P * k + P] for k in range(4 * q, 4 * q + 4)])
            for g in range(G):
                for q in range(2):
                    wait_emptied(pe, f"hT_{g}_{q}")

            def tokens(ap, d):
                ap = ap.rearrange("p (g t) -> p g t", g=G)
                return ap[:, :, ::-1] if d else ap

            def s5_in_mm(tp, d):
                if tp:
                    pe.wait_ge(bu_used, 2 * (tp - 1) + d + 1)
                pe.wait_ge(pad_ready, 2 * (2 * tp + d + 1))
                for i in range(2):
                    tile = 2 * tp + i
                    for r in range(2):
                        mm = pe.matmul(psum[:, 2 * d + i, 256 * r:256 * r + 256],
                                       pads[tile % 4][:, r, :], tokens(uT[:, tile // 4, :], d), start=True, stop=True)
                mm.then_inc(bu_ready, 1)

            def s5_in(tp):
                for d in range(2):
                    s5_in_mm(tp, d)

            arrived("in_u")
            w = weight("in_u", SSM)
            for c in range(NC):
                if c == 2:
                    pe.wait_ge(fb_ready, 1)
                    for i in range(4):
                        transposes(f"fb{i}", [fb[:, i // 2, 16 * (i % 2) + 4 * q:16 * (i % 2) + 4 * q + 4, :]
                                              .rearrange("p a c -> p (a c)") for q in range(4)])
                out = start(f"u{c // 2}") if c % 2 == 0 else out
                for k in range(KD):
                    mm = pe.matmul(out[:, 256 * (c % 2):256 * (c % 2) + 256], w[:, k, P * c:P * c + P], hT[:, k, :],
                                   start=k == 0, stop=k == KD - 1)
                if c % 2:
                    finish(mm, f"u{c // 2}")
                if c == 2:
                    wait_emptied(pe, "u0")
                    for i in range(4):
                        wait_emptied(pe, f"fb{i}")
                    s5_in(0)

            wq, wkv = weight("in_q", QR), weight("in_kv", KVR + ROPE)

            def query_latent(g):
                arrived("in_q")
                arrived("in_kv")
                out = start(f"cq{g}")
                for k in range(KD):
                    mm = pe.matmul(out[:, 0:QR], hT[:, k, P * g:P * g + P], wq[:, k, :], start=k == 0, stop=k == KD - 1)
                for k in range(KD):
                    mm = pe.matmul(out[:, QR:QR + ROPE], hT[:, k, P * g:P * g + P], wkv[:, k, KVR:KVR + ROPE],
                                   start=k == 0, stop=k == KD - 1)
                finish(mm, f"cq{g}")

            def key_latents():
                out = start("kv")
                for g in range(G):
                    for k in range(KD):
                        mm = pe.matmul(out[:, KVR * g:KVR * g + KVR], hT[:, k, P * g:P * g + P], wkv[:, k, 0:KVR],
                                       start=k == 0, stop=k == KD - 1)
                finish(mm, "kv")

            def s5_out_mm(tp, d):
                pe.wait_ge(qd_ready, 4 * tp + 2 * d + 2)
                pe.wait_ge(qp_ready, 4 * tp + 2 * d + 3)
                if d == 0 and tp in (0, 4):
                    start(f"y{tp // 4}")
                for k in range(4):
                    for i in range(2):
                        tile = 2 * tp + i
                        j, c = 32 * (tile % 4), tile // 4
                        mm = pe.matmul(psum[j:j + 32, 4 + c // 2, 256 * (c % 2):256 * (c % 2) + 256],
                                       (cm[:, 0], cneg, cm[:, 1], cm[:, 1])[k][:, TILES * d + tile, :],
                                       tokens(qm[:, d, k, 256 * i:256 * i + 256], d),
                                       start=d == 0 and k == 0, stop=d == 1 and k == 3, tile_position=(0, j))
                mm.then_inc(q_used, 1)

            pe.sem_inc(q_used, 1)

            def s5_out(tp):
                for d in range(2):
                    s5_out_mm(tp, d)

            def attention_queries(g, q):
                arrived("uq")
                w, out = weight("uq", HEADS * QK, 3), start(f"q_{g}_{q}")
                for k in range(3):
                    mm = pe.matmul(out[:, 0:384], cqT[:, g, k, :], w[:, k, 384 * q:384 * q + 384],
                                   start=k == 0, stop=k == 2)
                finish(mm, f"q_{g}_{q}")

            s5_in(1)
            query_latent(0)
            pe.wait_ge(s5c_ready, 2)
            s5_out(0)
            s5_in(2)
            query_latent(1)
            s5_out(1)
            s5_in(3)
            key_latents()
            wait_emptied(pe, "u1")
            for tp in range(2, TILES // 2):
                if tp in (4, 5, 7):
                    mod_pair(2 * tp - 4)
                if 3 <= tp < TILES // 2 - 1:
                    s5_in(tp + 1)
                if tp == 6:
                    mod_pair(2 * tp - 4)
                if tp == 7:
                    pe.wait_ge(cache_in, 16)
                    for b in range(3):
                        transposes(f"ckvT{b}", [ckvn[:, b, P * k:P * k + P] for k in range(2)])
                    for g in range(G):
                        wait_emptied(pe, f"cqT{g}")
                    pe.wait_ge(bu_used, TILES)
                    for q in range(2):
                        attention_queries(0, q)
                s5_out(tp)
                if tp == 6:
                    for g in range(G):
                        transposes(f"cqT{g}", [cqn[:, g, P * k:P * k + P] for k in range(3)])
                if tp % 4 == 3:
                    pe.wait_ge(q_used, 2 * tp + 3)
                    pe.sem_inc(filled[4 + tp // 4], 1)
            pe.wait_ge(last_ready, 2 * TILES + 1)
            finish(pe.transpose(start("hlast")[0:2 * DT, 0:P], hlast, ident[:, :]), "hlast")

            for q in range(2):
                attention_queries(1, q)
            pe.wait_ge(yg_ready, 2)
            arrived("glu")
            w = weight("glu", SSM, 4)
            for c in range(NC):
                out = start(f"glu{c // 2}") if c % 2 == 0 else out
                for k in range(4):
                    mm = pe.matmul(out[:, 256 * (c % 2):256 * (c % 2) + 256], w[:, k, P * c:P * c + P], ygT[:, k, :],
                                   start=k == 0, stop=k == 3)
                if c % 2:
                    finish(mm, f"glu{c // 2}")

            for b in range(3):
                wait_emptied(pe, f"ckvT{b}")
            arrived("ukv")
            w = weight("ukv", 512, 4)
            for m, name in enumerate("kv"):
                for b in range(3):
                    out = start(f"{name}{b}")
                    for k in range(2):
                        mm = pe.matmul(out, ckvT[b][:, k, :], w[:, 2 * m + k, :], start=k == 0, stop=k == 1)
                    finish(mm, f"{name}{b}")
            for g in range(G):
                pe.wait_ge(q_ready, g + 1)
                for q in range(2):
                    transposes(f"qT_{g}_{q}", [qtok[:, g, a, :] for a in range(4 * q, 4 * q + 4)], QK)
            pe.wait_ge(k_ready, 3)
            for b in range(3):
                wait_emptied(pe, f"k{b}")
                for q in range(2):
                    transposes(f"kT_{b}_{q}", [ktok[:, b, a, :] for a in range(4 * q, 4 * q + 4)], QK)
            for b in range(3):
                for q in range(2):
                    wait_emptied(pe, f"kT_{b}_{q}")
            for g in range(G):
                per, nb_, b0 = (4, 1, 0) if g == 0 else (2, 2, 1)
                wait_emptied(pe, f"qT_{g}_0")
                wait_emptied(pe, f"qT_{g}_1")
                for q in range(2 + 2 * g):
                    out = start(f"s_{g}_{q}")
                    for a in range(per):
                        mm = pe.matmul(out[:, nb_ * P * a:nb_ * P * (a + 1)], qT[0:QK, g, per * q + a, :],
                                       kT[0:QK, per * q + a, b0:b0 + nb_, :], start=True, stop=True)
                    finish(mm, f"s_{g}_{q}")
            for b in range(3):
                wait_emptied(pe, f"v{b}")
            def attended(g):
                pe.wait_ge(probs_ready, g + 1)
                for q in range(2 + 2 * g):
                    transposes(f"pT_{g}_{q}", [probs[:, P * i:P * i + P] for i in range(4 * q, 4 * q + 4)])
                for q in range(2 + 2 * g):
                    wait_emptied(pe, f"pT_{g}_{q}")
                out = start(f"at{g}")
                for pair in range(HEADS // 2):
                    for b in range(1 + g):
                        for r in (0, VD):
                            a = 2 * pair + r // VD
                            mm = pe.matmul(out[r:r + VD, P * pair:P * pair + P],
                                           vtok[:, g + b, VD * a:VD * a + VD], prT[:, (1 + g) * a + b, :],
                                           start=b == 0, stop=b == g, tile_position=(0, r))
                finish(mm, f"at{g}")

            def out_projection(g):
                pe.wait_ge(ssm_ready, 2)
                for half in range(2):
                    arrived(f"out{half}")
                    w, out = weight(f"out{half}", 512), start(f"mix_{g}_{half}")
                    for k in range(KD):
                        if k == 4:
                            wait_emptied(pe, f"at{g}")
                        mm = pe.matmul(out, mixT[:, k, P * g:P * g + P], w[:, k, :], start=k == 0, stop=k == KD - 1)
                    finish(mm, f"mix_{g}_{half}")

            def h2_transposed(g):
                pe.wait_ge(h2_ready, g + 1)
                for q in range(2):
                    transposes(f"h2T_{g}_{q}", [h[:, g, P * k:P * k + P] for k in range(4 * q, 4 * q + 4)])
                for q in range(2):
                    wait_emptied(pe, f"h2T_{g}_{q}")

            def queries(g, n):
                arrived(f"query{n}")
                w, out = weight(f"query{n}", 512), start(f"qry_{g}_{n}")
                for i in range(4):
                    for k in range(KD):
                        mm = pe.matmul(out[:, P * i:P * i + P], w[:, k, P * i:P * i + P], hT[:, k, P * g:P * g + P],
                                       start=k == 0, stop=k == KD - 1)
                finish(mm, f"qry_{g}_{n}")

            def scores(g, n):
                wait_emptied(pe, f"qry_{g}_{n}")
                out = start(f"sc_{g}_{n}")
                for i in range(4):
                    mm = pe.matmul(out[:, P * i:P * i + P], qryT[:, (2 * n + g) % 4, i, :], keys_sb[:, 4 * n + i, :],
                                   start=True, stop=True)
                finish(mm, f"sc_{g}_{n}")

            def accumulate(g, it, first=False, last=False):
                if first:
                    for half in range(2):
                        start(f"acc_{g}_{half}")
                for k in range(BATCH):
                    pe.wait_ge(diag_ready, BATCH * it + (k + 2))
                    pe.wait_ge(v_landed[k], 16 * (it + 1))
                    for half in range(2):
                        mm = pe.matmul(bank(f"acc_{g}_{half}"), diag[:, k, :], v_rows[k][:, 512 * half:512 * half + 512],
                                       start=first and k == 0, stop=last and k == BATCH - 1)
                        if last and k == BATCH - 1:
                            finish(mm, f"acc_{g}_{half}")
                    if not (last and k == BATCH - 1):
                        mm.then_inc(v_free, 1)

            attended(0)
            out_projection(0)
            attended(1)
            out_projection(1)
            h2_transposed(0)
            queries(0, 0)
            pe.wait_ge(keys_in, 16)
            scores(0, 0)
            h2_transposed(1)
            queries(1, 0)
            scores(1, 0)
            wait_filled(pe, "qry_1_0")
            pe.sem_inc(v_free, BATCH // 2)
            for n in range(1, 4):
                for g in range(G):
                    queries(g, n)
                for g in range(G):
                    scores(g, n)
                if n == 1:
                    wait_filled(pe, "qry_1_1")
                    pe.sem_inc(v_free, BATCH // 2)
                if n == 2:
                    accumulate(0, 0, first=True)

            for g in range(G):
                if g:
                    accumulate(g, NB, first=True)
                with pe.Fori(NB * g + 1, NB * g + NB - 1) as it:
                    accumulate(g, it)
                accumulate(g, NB * g + NB - 1, last=True)
                if g == 0:
                    wait_filled(pe, "acc_0_1")
                    pe.sem_inc(v_free, 1)

        @block.scalar
        def _(act):
            n = [0]

            def step(ins):
                n[0] += 1
                ins.then_inc(act_step, 1)
                act.wait_ge(act_step, n[0])

            def evacuate(dst, src, name, last=True):
                wait_filled(act, name)
                ins = act.copy(dst, src)
                if last:
                    empties(ins, name)

            act.wait_ge(c_in, 16)
            act.activation(scol[:, :, :], ccol[:, :, :], ACT.Silu).then_inc(silu_ready, 1)
            act.wait_ge(s5_in, 32)
            act.activation(dtv, ldt, ACT.Exp).then_inc(dt_ready, 1)
            act.wait_ge(lr_ready, 1)
            act.activation(rad, t0, ACT.Exp).then_inc(r_ready, 1)

            def mod_evac(m):
                j = 32 * (m % 4)
                evacuate(modrow[j:j + G, m // 4, :], bank(f"mod{m}")[j:j + G, :], f"mod{m}")
            act.wait_ge(pool_step, 2)
            for m in range(3):
                mod_evac(m)
            act.wait_ge(angle_ready, 1)
            act.activation(one_step[:, :, :], arena[:, 0:8192].rearrange("p (c a t) -> p c a t", c=2, t=P)[:, :, :, 1],
                           ACT.Sin, scale=6.283185).then_inc(first_ready, 1)
            mod_evac(3)
            act.wait_ge(first_ready, 1)
            act.activation(arena[:, 0:8192], arena[:, 0:8192], ACT.Sin, scale=6.283185).then_inc(tab_ready, 1)

            def soft_exp(u):
                act.wait_ge(best_ready, u + 1)
                cut = gate[:, bass.ds(UP * u, UP)]
                act.activation(cut, cut, ACT.Exp).then_inc(gexp_ready, 1)

            for g in range(G):
                for q in range(2):
                    evacuate(hT[:, 4 * q:4 * q + 4, P * g:P * g + P], bank(f"hT_{g}_{q}").rearrange("p (k n) -> p k n", k=4),
                             f"hT_{g}_{q}")
            def input_evac(i):
                evacuate(uT[:, 2 * i:2 * i + 2, :], bank(f"u{i}"), f"u{i}")

            def square(src, width, col, count):
                act.activation(junk5[:, 0:width], src, ACT.Square, accum_out=ms_a[:, col:col + 1]).then_inc(sq_ready, 1)
                act.wait_ge(sq_ready, count)

            def fill_pads(tp, d):
                if d:
                    act.wait_ge(bu_ready, 2 * tp + 1)
                elif tp >= 2:
                    act.wait_ge(bu_ready, 2 * (tp - 1))
                for i in range(2):
                    tile = 2 * tp + i
                    j = tile % 4
                    act.copy(pads[j][32 * j:32 * j + 32, :, :],
                             fbT[32 * j:32 * j + 32, d * 4 + tile // 4:16:8, :]).then_inc(pad_ready, 1)

            input_evac(0)
            for i in range(4):
                evacuate(fbT[:, 4 * i:4 * i + 4, :], bank(f"fb{i}"), f"fb{i}")
            for i in range(4):
                wait_emptied(act, f"fb{i}")
            act.wait_ge(pad_zero, 1)
            fill_pads(0, 0)
            fill_pads(0, 1)
            fill_pads(1, 0)
            input_evac(1)
            fill_pads(1, 1)
            fill_pads(2, 0)
            wait_filled(act, "cq0")
            square(bank("cq0")[:, 0:QR], QR, 0, 3)
            fill_pads(2, 1)
            fill_pads(3, 0)
            wait_filled(act, "cq1")
            square(bank("cq1")[:, 0:QR], QR, 1, 4)
            fill_pads(3, 1)
            wait_filled(act, "kv")
            for g in range(G):
                square(bank("kv")[:, KVR * g:KVR * g + KVR], KVR, 2 + g, 5 + g)
            for tp in range(4, TILES // 2):
                for d in range(2):
                    fill_pads(tp, d)
                if tp == 5:
                    act.wait_ge(krope_ready, 1)
                    act.wait_ge(latent_ready, 2)
                    act.dma_start(new_ckv, ckvn[:, 0, :]).then_inc(stored, 16)
                    act.dma_start(new_krope, krope[:, 0, :]).then_inc(stored, 16)
                if tp >= 5:
                    for m in (2 * tp - 6, 2 * tp - 5):
                        mod_evac(m)
            for g in range(G):
                evacuate(cqT[:, g, :, :], bank(f"cqT{g}")[:, 0:QR].rearrange("p (k n) -> p k n", k=3), f"cqT{g}")
            for m in (10, 11):
                mod_evac(m)
            act.wait_ge(q_used, 2 * 6 + 1)
            for b in range(3):
                evacuate(ckvT[b], bank(f"ckvT{b}")[:, 0:KVR].rearrange("p (k n) -> p k n", k=2), f"ckvT{b}")
            evacuate(hlT, bank("hlast")[0:2 * DT, 0:P], "hlast")
            wait_emptied(act, "hlast")
            act.dma_start(new_ssm, hlT).then_inc(stored, 16)
            for i in range(2):
                act.wait_ge(y_ready, i + 1)
                act.activation(ygT[:, 2 * i:2 * i + 2, :], yT[:, 2 * i:2 * i + 2, :], ACT.Gelu_apprx_tanh).then_inc(yg_ready, 1)
            for i in range(2):
                wait_filled(act, f"glu{i}")
                empties(act.activation(sgT[:, 2 * i:2 * i + 2, :], bank(f"glu{i}"), ACT.Sigmoid), f"glu{i}")
            for b in range(3):
                evacuate(ktok[:, b, :, 0:NOPE], bank(f"k{b}").rearrange("p (a d) -> p a d", a=HEADS), f"k{b}")
            for b in range(3):
                evacuate(vtok[:, b, :], bank(f"v{b}"), f"v{b}")
            for b in range(3):
                for q in range(2):
                    evacuate(kT[0:QK, 4 * q:4 * q + 4, b, :],
                             bank(f"kT_{b}_{q}")[0:QK, :].rearrange("p (a n) -> p a n", a=4), f"kT_{b}_{q}")
            for g in range(G):
                per, nb_ = (4, 1) if g == 0 else (2, 2)
                act.wait_ge(nb_ready, g + 1)
                if g:
                    wait_filled(act, "pT_0_1")
                for a in range(HEADS):
                    w = nb_ * P
                    ins = act.activation(probs[:, w * a:w * a + w],
                                         bank(f"s_{g}_{a // per}")[:, w * (a % per):w * (a % per) + w], ACT.Exp,
                                         bias=nb[:, a:a + 1], scale=SCALE, accum_out=rs[:, a:a + 1])
                    if a % per == per - 1:
                        empties(ins, f"s_{g}_{a // per}")
                    else:
                        step(ins)
                for q in range(2 + 2 * g):
                    evacuate(prT[:, 4 * q:4 * q + 4, :], bank(f"pT_{g}_{q}").rearrange("p (a n) -> p a n", a=4),
                             f"pT_{g}_{q}")
                act.wait_ge(stored, 3 * 16)
                evacuate(mixT[:, 4:8, P * g:P * g + P], bank(f"at{g}").rearrange("p (a n) -> p a n", a=4), f"at{g}")
            def turned(g):
                for q in range(2):
                    evacuate(hT[:, 4 * q:4 * q + 4, P * g:P * g + P],
                             bank(f"h2T_{g}_{q}").rearrange("p (k n) -> p k n", k=4), f"h2T_{g}_{q}")

            def scored(g, n):
                cut = s_sb[:, 2048 * g + 512 * n:2048 * g + 512 * n + 512]
                evacuate(cut, bank(f"sc_{g}_{n}"), f"sc_{g}_{n}")
                wait_emptied(act, f"sc_{g}_{n}")
                act.sem_inc(scores_ready, 1)

            def query(g, n):
                if n >= 2:
                    wait_filled(act, f"sc_{g}_{n - 2}")
                evacuate(qryT[:, (2 * n + g) % 4, :, :], bank(f"qry_{g}_{n}").rearrange("p (i n) -> p i n", i=4), f"qry_{g}_{n}")

            act.sem_inc(gel_ready, 1)
            act.sem_inc(diag_ready, 1)
            def weigh(it):
                act.wait_ge(u_free, BATCH * (it + 2))
                act.activation(gel[:, 0:BATCH], dots[:, 0:BATCH], ACT.Gelu_apprx_tanh).then_inc(gel_ready, 1)
                act.wait_ge(wts_ready, it + 1)
                for k in range(BATCH):
                    act.wait_ge(v_free, BATCH * it + (k + 1))
                    act.activation(diag[:, k, :], ident[:, :], ACT.Copy, scale=wts[:, k:k + 1]).then_inc(diag_ready, 1)

            turned(0)
            query(0, 0)
            scored(0, 0)
            turned(1)
            query(1, 0)
            scored(1, 0)
            for n in range(1, 4):
                if n == 3:
                    weigh(1)
                query(0, n)
                if n == 2:
                    weigh(0)
                query(1, n)
                for g in range(G):
                    scored(g, n)
                soft_exp(n - 1)
            with act.Fori(1, UNITS - 2) as j:
                weigh(2 * j)
                soft_exp(j + 2)
                weigh(2 * j + 1)
            with act.Fori(2 * (UNITS - 2), 2 * NB) as it:
                weigh(it)

        @block.gpsimd
        def _(pool):
            n = [0]

            def step(ins):
                n[0] += 1
                ins.then_inc(pool_step, 1)
                pool.wait_ge(pool_step, n[0])

            step(pool.memset(brow[:, :, :], 0.0))
            step(pool.memset(modrow[:, :, :], 0.0))
            step(pool.memset(half_neg[:, :], -0.5))
            step(pool.memset(pads3[:, :, :, :], 0.0))

            def inverse_root(out, src, width, ready, signal):
                pool.wait_ge(*ready)
                for lo, hi, w in width:
                    step(pool.tensor_scalar(src[:, lo:hi], src[:, lo:hi], 1.0 / w, EPS, ALU.mult, ALU.add))
                pool.tensor_tensor(out, src, half_neg[:, 0:src.shape[1]], ALU.pow).then_inc(signal, 1)

            inverse_root(rstd, ms, [(0, 2, D)], (sq_ready, 2), rstd_ready)
            for g in range(G):
                wait_filled(pool, f"hT_{g}_1")
            pool.memset(pads[0], 0.0).then_inc(pad_zero, 1)
            pool.wait_ge(late_in, 4 * 16)
            for dst, src in ((cneg, cm[:, 0, :, :]), (cm[:, 1, :, :], cm[:, 1, :, :])):
                pool.tensor_scalar(dst, src, -1.0, 0.0, ALU.mult, ALU.add).then_inc(s5c_ready, 1)

            for counted in (v_ready, qp_ready, last_ready):
                pool.sem_inc(counted, 1)
            def pairs(first, last):
                with pool.Fori(first, last) as tp:
                    for d in range(2):
                        pool.wait_ge(prod_ready, 8 * tp + (4 * d + 2))
                        pool.tensor_tensor(vm[:, d, 0, :], pm[:, d, 0, :], pm[:, d, 1, :], ALU.add).then_inc(v_ready, 1)
                        pool.wait_ge(prod_ready, 8 * tp + (4 * d + 4))
                        pool.tensor_tensor(vm[:, d, 1, :], pm[:, d, 2, :], pm[:, d, 3, :], ALU.subtract).then_inc(v_ready, 1)
                    for d in range(2):
                        pool.wait_ge(g_ready, 16 * tp + (8 * d + 8))
                        pool.wait_ge(q_used, 2 * tp + 1)
                        for k, tab, r in ((2, sin_t, 0), (3, cos_t, 1)):
                            ins = pool.tensor_tensor(
                                qm[:, d, k, :].rearrange("p (i g t) -> p i g t", i=2, g=G),
                                gm[:, d, r, :].rearrange("p (i g t) -> p i g t", i=2, g=G),
                                tab[:, bass.ds(TILES * d + 2 * tp, 2), :].unsqueeze(2).to_broadcast([P, 2, G, P]), ALU.mult)
                            ins.then_inc(qp_ready, 1)
                        pool.wait_ge(qd_ready, 4 * tp + (2 * d + 2))
                        pool.wait_ge(qp_ready, 4 * tp + (2 * d + 3))
                        for r, op in ((0, ALU.subtract), (1, ALU.add)):
                            a_, b_ = (qm[:, d, 2 * r + e, :].rearrange("p (i n) -> p i n", i=2)[:, :, P - 1] for e in range(2))
                            pool.tensor_tensor(hlast[:, bass.ds(TILES * (2 * d + r) + 2 * tp, 2)], a_, b_,
                                               op).then_inc(last_ready, 1)

            pairs(0, 3)
            inverse_root(rstd_a, ms_a, [(0, 2, QR), (2, 4, KVR)], (sq_ready, 6), rstd_ready)
            pairs(3, TILES // 2)

            wait_emptied(pool, "hlast")
            for b in range(3):
                pool.tensor_copy(ktok[:, b, :, NOPE:QK], krope[:, b:b + 1, :].to_broadcast([P, HEADS, ROPE])).then_inc(k_ready, 1)

            for g in range(G):
                inverse_root(rstd_2[:, g:g + 1], ms_2[:, g:g + 1], [(0, 1, D)], (sq2_ready, g + 1), rstd2_ready)

            with pool.Fori(0, NB) as i:
                pool.wait_ge(idx_ready, i + 1)
                for half in range(2):
                    it = 2 * i + half
                    st = stage[:, BATCH * half:BATCH * half + BATCH]
                    pool.tensor_copy(st, idx[:, bass.ds(2 * BATCH * i + BATCH * half, BATCH)]).then_inc(staged, 1)
                    pool.wait_ge(staged, it + 1)
                    pool.sem_inc(stepped, 1)
                    for table, used, sems, rows in ((u_table, u_free, u_landed, u_rows), (v_table, v_free, v_landed, v_rows)):
                        for k in range(BATCH):
                            pool.wait_ge(used, BATCH * it + (k + 1))
                            pool.sem_inc(stepped, 1)
                            pool.indirect_dma_start(rows[k], None, table,
                                                    bass.IndirectOffsetOnAxis(ap=st[:, k:k + 1], axis=0)).then_inc(sems[k], 16)
            for g in range(G):
                inverse_root(rstd_f[:, g:g + 1], ms_f[:, g:g + 1], [(0, 1, D)], (sqf_ready, g + 1), rstdf_ready)

        @block.vector
        def _(dve):
            n = [0]

            def step(ins):
                n[0] += 1
                ins.then_inc(dve_step, 1)
                dve.wait_ge(dve_step, n[0])

            def tt(out, a, b, op):
                step(dve.tensor_tensor(out, a, b, op))

            dve.wait_ge(dt_ready, 1)
            dve.wait_ge(s5_in, 32)
            dve.tensor_tensor(t0, lre, dtv, ALU.mult).then_inc(lr_ready, 1)
            tt(turns, lim, dtv, ALU.mult)
            step(dve.tensor_scalar(kturn, turns, INV_2PI, MAGIC, ALU.mult, ALU.add))
            step(dve.tensor_scalar(kturn, kturn, MAGIC, None, ALU.subtract))
            step(dve.scalar_tensor_tensor(turns, kturn, -C1, turns, ALU.mult, ALU.add))
            step(dve.scalar_tensor_tensor(turns, kturn, -C2, turns, ALU.mult, ALU.add))
            step(dve.tensor_scalar(turns, turns, INV_2PI, None, ALU.mult))
            tt(sin_t, turns.unsqueeze(2).to_broadcast([P, DT, P]), iota[:, :].unsqueeze(1).to_broadcast([P, DT, P]), ALU.mult)
            step(dve.tensor_scalar(cos_t, sin_t, MAGIC, MAGIC, ALU.add, ALU.subtract))
            tt(sin_t, sin_t, cos_t, ALU.subtract)
            step(dve.tensor_scalar(cos_t, sin_t, 0.25, None, ALU.is_gt))
            dve.scalar_tensor_tensor(cos_t, sin_t, 0.25, cos_t, ALU.add, ALU.subtract).then_inc(angle_ready, 1)
            dve.wait_ge(angle_ready, 1)
            dve.wait_ge(first_ready, 1)
            dve.wait_ge(r_ready, 1)
            s1, c1 = one_step[:, 0, :], one_step[:, 1, :]
            tt(are, rad, c1, ALU.mult)
            tt(aim, rad, s1, ALU.mult)
            tt(t0, lre, lre, ALU.mult)
            tt(t1, lim, lim, ALU.mult)
            tt(t0, t0, t1, ALU.add)
            step(dve.reciprocal(rden, t0))
            step(dve.tensor_scalar(are, are, -1.0, None, ALU.add))
            tt(t0, are, lre, ALU.mult)
            tt(t1, aim, lim, ALU.mult)
            tt(t0, t0, t1, ALU.add)
            tt(fre, t0, rden, ALU.mult)
            tt(t0, aim, lre, ALU.mult)
            tt(t1, are, lim, ALU.mult)
            tt(t0, t0, t1, ALU.subtract)
            dve.tensor_tensor(fim, t0, rden, ALU.mult).then_inc(f_ready, 1)
            dve.wait_ge(f_ready, 1)
            dve.wait_ge(cst_in, 80)
            for m in range(4):
                wait_emptied(dve, f"mod{m}")
            dve.wait_ge(pool_step, 2)
            dve.tensor_tensor(modrow[:, 0, :], modrow[:, 0, :], brow[:, 0, :], ALU.add).then_inc(modrow_ready, 1)
            dve.wait_ge(x_in, 32)
            for g in range(G):
                dve.tensor_tensor_reduce(out=junk1, in0=x[:, g, :], in1=x[:, g, :], scale=1.0, scalar=0.0,
                                         op0=ALU.mult, op1=ALU.add, accum_out=ms[:, g:g + 1]).then_inc(sq_ready, 1)
                dve.wait_ge(sq_ready, g + 1)

            def modulated(g, scale_, shift, norm, tmp, root, signal):
                for half in range(2):
                    cut = slice(512 * half, 512 * half + 512)
                    name = f"bc_{scale_}_{g}_{half}"
                    wait_filled(dve, name)
                    ins = dve.scalar_tensor_tensor(tmp[:, cut], bank(name), 1.0, norm[:, cut], ALU.add, ALU.mult)
                    empties(ins, name)
                    wait_emptied(dve, name)
                step(dve.scalar_tensor_tensor(h[:, g, :], x[:, g, :], root[:, g:g + 1], tmp, ALU.mult, ALU.mult))
                for half in range(2):
                    cut = slice(512 * half, 512 * half + 512)
                    name = f"bc_{shift}_{g}_{half}"
                    wait_filled(dve, name)
                    empties(dve.tensor_tensor(h[:, g, cut], h[:, g, cut], bank(name), ALU.add), name)
                    wait_emptied(dve, name)
                dve.sem_inc(signal, 1)

            dve.wait_ge(rstd_ready, 1)
            dve.wait_ge(n1_in, 16)
            for g in range(G):
                modulated(g, "sc1", "sh1", n1b, tmpA, rstd, h_ready)

            dve.wait_ge(b_in, 32)
            def spread(v):
                return v.unsqueeze(2).to_broadcast([P, DT, 32])
            for r, (first, second, op) in enumerate(((fre, fim, ALU.subtract), (fim, fre, ALU.add))):
                tt(fbt1, bm[:, 0, :, :], spread(first), ALU.mult)
                tt(fbt2, bm[:, 1, :, :], spread(second), ALU.mult)
                ins = dve.tensor_tensor(fb[:, r, :, :], fbt1, fbt2, op)
                if r == 0:
                    step(ins)
                else:
                    ins.then_inc(fb_ready, 1)
            hr, hi = h0_sb[:, 0:DT], h0_sb[:, DT:2 * DT]
            for r, (a_, b_, op) in enumerate(((c1, s1, ALU.subtract), (s1, c1, ALU.add))):
                tt(t0, hr, a_, ALU.mult)
                tt(t1, hi, b_, ALU.mult)
                tt(init[:, DT * r:DT * r + DT], t0, t1, op)

            def rotary(dst, src, tmp, heads, tail):
                cs = rope[:, 0:1, :].to_broadcast([P, heads, ROPE])
                sn = rope[:, 1:2, :].to_broadcast([P, heads, ROPE])
                step(dve.tensor_tensor(tmp[:, 0], src, cs, ALU.mult))
                for r in range(2):
                    for s_ in range(2):
                        at_, of = 16 * r + 8 * s_, 16 * r + 8 * (1 - s_)
                        step(dve.tensor_tensor(tmp[:, 1, :, at_:at_ + 8], src[:, :, of:of + 8], sn[:, :, at_:at_ + 8], ALU.mult))
                tail(dve.tensor_tensor(dst, tmp[:, 0], tmp[:, 1], ALU.add))

            def latents():
                dve.wait_ge(rstd_ready, 2)
                dve.wait_ge(late_in, 4 * 16)
                dve.wait_ge(norm_in, 2 * 16)
                wait_filled(dve, "kv")
                for g in range(G):
                    wait_filled(dve, f"cq{g}")
                    step(dve.tensor_copy(krope[:, 2 * g, :], bank(f"cq{g}")[:, QR:QR + ROPE]))
                    empties(dve.scalar_tensor_tensor(cqn[:, g, :], bank(f"cq{g}")[:, 0:QR], rstd_a[:, g:g + 1], qnb,
                                                     ALU.mult, ALU.mult), f"cq{g}")
                    ins = dve.scalar_tensor_tensor(ckvn[:, 2 * g, :], bank("kv")[:, KVR * g:KVR * g + KVR],
                                                   rstd_a[:, 2 + g:3 + g], kvb, ALU.mult, ALU.mult)
                    if g == 0:
                        step(ins)
                    else:
                        empties(ins, "kv")
                rotary(krope[:, 2:3, :], krope[:, 2:3, :], krt, 1, lambda ins: ins.then_inc(krope_ready, 1))
                dve.wait_ge(krope_ready, 1)
                for m in ("cq0", "cq1", "kv"):
                    wait_emptied(dve, m)
                dve.sem_inc(latent_ready, 2)

            def view(ap):
                return ap.rearrange("p (i g t) -> p i g t", i=2, g=G)
            dve.wait_ge(fb_ready, 1)
            dve.wait_ge(tab_ready, 1)

            def pairs(first, last):
                with dve.Fori(first, last) as tp:
                    def table(tab, d):
                        return tab[:, bass.ds(TILES * d + 2 * tp, 2), :].unsqueeze(2).to_broadcast([P, 2, G, P])
                    for d in range(2):
                        dve.wait_ge(bu_ready, 2 * tp + (d + 1))
                        dve.wait_ge(v_ready, 4 * tp + 1)
                        bu = psum[:, 2 * d:2 * d + 2, :].rearrange("p i (r g t) -> p r i g t", r=2, g=G)
                        for k, (r, tab) in enumerate(((0, cos_t), (1, sin_t), (1, cos_t), (0, sin_t))):
                            ins = dve.tensor_tensor(view(pm[:, d, k, :]), bu[:, r], table(tab, d), ALU.mult)
                            ins.then_inc(prod_ready, 1)
                        dve.wait_ge(prod_ready, 8 * tp + (4 * d + 4))
                        dve.sem_inc(bu_used, 1)
                    for d in range(2):
                        dve.wait_ge(qp_ready, 4 * tp + 1)
                        for r in range(2):
                            dve.wait_ge(v_ready, 4 * tp + (2 * d + r + 2))
                            for i in range(2):
                                for g in range(G):
                                    cut = slice(256 * i + P * g, 256 * i + P * g + P)
                                    start_ = init[:, bass.ds(DT * r + TILES * d + 2 * tp + i, 1)] if g else 0.0
                                    dve.tensor_tensor_scan(
                                        gm[:, d, r, cut], rad[:, bass.ds(TILES * d + 2 * tp + i, 1)].to_broadcast([P, P]),
                                        vm[:, d, r, cut], start_, ALU.mult, ALU.add).then_inc(g_ready, 1)
                        dve.wait_ge(g_ready, 16 * tp + (8 * d + 8))
                        dve.wait_ge(q_used, 2 * tp + 1)
                        dve.wait_ge(last_ready, 4 * tp + 1)
                        for k, (r, tab) in enumerate(((0, cos_t), (1, sin_t))):
                            dve.tensor_tensor(view(qm[:, d, k, :]), view(gm[:, d, r, :]), table(tab, d),
                                              ALU.mult).then_inc(qd_ready, 1)

            pairs(0, 4)
            latents()
            pairs(4, TILES // 2)

            for i in range(2):
                wait_filled(dve, f"y{i}")
                for c in (2 * i, 2 * i + 1):
                    ins = dve.scalar_tensor_tensor(yT[:, c, :], uT[:, c, :], dcol[:, c:c + 1],
                                                   bank(f"y{i}")[:, 256 * (c % 2):256 * (c % 2) + 256], ALU.mult, ALU.add)
                    if c % 2:
                        empties(ins, f"y{i}")
                    else:
                        step(ins)
                wait_emptied(dve, f"y{i}")
                dve.sem_inc(y_ready, 1)
            for m in range(4, 12):
                wait_emptied(dve, f"mod{m}")
            dve.tensor_tensor(modrow[:, 1:3, :], modrow[:, 1:3, :], brow[:, 1:3, :], ALU.add).then_inc(modrow_ready, 1)
            for g in range(G):
                for q in range(2):
                    name = f"q_{g}_{q}"
                    wait_filled(dve, name)
                    src = bank(name)[:, 0:384].rearrange("p (a d) -> p a d", a=4)
                    dst = qtok[:, g, 4 * q:4 * q + 4, :]
                    if g == 0:
                        empties(dve.tensor_copy(dst, src), name)
                    else:
                        step(dve.tensor_copy(dst[:, :, 0:NOPE], src[:, :, 0:NOPE]))
                        rotary(dst[:, :, NOPE:QK], src[:, :, NOPE:QK], rt[:, :, 4 * q:4 * q + 4, :], 4,
                               lambda ins: empties(ins, name))
                    wait_emptied(dve, name)
                dve.sem_inc(q_ready, 1)
            for i in range(2):
                wait_emptied(dve, f"glu{i}")
                dve.tensor_tensor(mixT[:, 2 * i:2 * i + 2, :], ygT[:, 2 * i:2 * i + 2, :], sgT[:, 2 * i:2 * i + 2, :],
                                  ALU.mult).then_inc(ssm_ready, 1)
            for g in range(G):
                for q in range(2):
                    wait_filled(dve, f"qT_{g}_{q}")
                    empties(dve.tensor_copy(qT[0:QK, g, 4 * q:4 * q + 4, :],
                                            bank(f"qT_{g}_{q}")[0:QK, :].rearrange("p (a n) -> p a n", a=4)), f"qT_{g}_{q}")
            def softmax(g):
                per = 4 if g == 0 else 2
                for q in range(2 + 2 * g):
                    wait_filled(dve, f"s_{g}_{q}")
                    step(dve.tensor_reduce(mx[:, per * q:per * q + per],
                                           bank(f"s_{g}_{q}").rearrange("p (a n) -> p a n", a=per), AX.X, ALU.max))
                dve.tensor_scalar(nb, mx, -SCALE, None, ALU.mult).then_inc(nb_ready, 1)
                for q in range(2 + 2 * g):
                    wait_emptied(dve, f"s_{g}_{q}")
                step(dve.reciprocal(rr, rs))
                pv = probs[:, 0:HEADS * P * (1 + g)].rearrange("p (a n) -> p a n", a=HEADS)
                dve.tensor_tensor(pv, pv, rr.unsqueeze(2).to_broadcast([P, HEADS, P * (1 + g)]),
                                  ALU.mult).then_inc(probs_ready, 1)

            def residual(g):
                for half in range(2):
                    name, cut = f"mix_{g}_{half}", slice(512 * half, 512 * half + 512)
                    wait_filled(dve, name)
                    empties(dve.tensor_tensor(tmpB[:, cut], bank(name), g1b[:, g, cut], ALU.mult), name)
                    wait_emptied(dve, name)
                    tt(x[:, g, cut], x[:, g, cut], tmpB[:, cut], ALU.add)
                dve.tensor_tensor_reduce(out=junk2, in0=x[:, g, :], in1=x[:, g, :], scale=1.0, scalar=0.0,
                                         op0=ALU.mult, op1=ALU.add, accum_out=ms_2[:, g:g + 1]).then_inc(sq2_ready, 1)
                dve.wait_ge(sq2_ready, g + 1)

            def norm2_of(g):
                dve.wait_ge(rstd2_ready, g + 1)
                step(dve.scalar_tensor_tensor(h[:, g, :], x[:, g, :], rstd_2[:, g:g + 1], sc2b[:, g, :], ALU.mult, ALU.mult))
                dve.tensor_tensor(h[:, g, :], h[:, g, :], sh2b[:, g, :], ALU.add).then_inc(h2_ready, 1)

            softmax(0)
            softmax(1)
            for v in ("sc2", "sh2", "g1"):
                dve.wait_ge(rows_in[v], 64)
            dve.wait_ge(n2_in, 16)
            for g in range(G):
                step(dve.scalar_tensor_tensor(sc2b[:, g, :], sc2b[:, g, :], 1.0, n2b, ALU.add, ALU.mult))
            residual(0)
            norm2_of(0)
            residual(1)
            norm2_of(1)
            dve.wait_ge(h2_ready, 2)

            def find(u, heads=(0, 2)):
                dve.wait_ge(scores_ready, 2 * (u % 4) + u // 4 + 1)
                lo, hi = heads
                n, tables = hi - lo, slice(2 * lo, 2 * hi)
                rows = [s_sb[:, NKEYS * (4 * u + r):NKEYS * (4 * u + r + 1)] for r in range(2 * lo, 2 * hi)]
                top16(rows, s2, tops[:, tables], topi[:, tables])
                step(dve.tensor_copy(topf[:, tables], topi[:, tables]))
                pair = tops[:, tables].rearrange("p (a r) n -> p a r n", r=2)
                wide = [P, n, TOPK, TOPK]
                step(dve.tensor_tensor(cand[:, lo:hi].rearrange("p a (i j) -> p a i j", i=TOPK),
                                       pair[:, :, 0, :].unsqueeze(3).to_broadcast(wide),
                                       pair[:, :, 1, :].unsqueeze(2).to_broadcast(wide), ALU.add))
                top16([cand[:, a, :] for a in range(lo, hi)], cand2, best[:, lo:hi], pos[:, lo:hi])
                ins = dve.tensor_tensor(gates(u)[:, lo:hi], best[:, lo:hi], best[:, lo:hi, 0:1].to_broadcast([P, n, TOPK]),
                                        ALU.subtract)
                if hi == 2:
                    ins.then_inc(best_ready, 1)
                else:
                    step(ins)

            def top16(rows, spare, out_v, out_i):
                for first in (0, 8):
                    src = rows if first == 0 else [spare[:, r, :] for r in range(len(rows))]
                    for r, row in enumerate(src):
                        last = dve.max(out_v[:, r, first:first + 8], row)
                    step(last)
                    for r, row in enumerate(src):
                        last = dve.max_index(out_i[:, r, first:first + 8], out_v[:, r, first:first + 8], row)
                        if first == 0:
                            last = dve.match_replace(spare[:, r, :], out_v[:, r, 0:8], row, LOW)
                    step(last)

            def gates(u):
                return gate[:, UP * u:UP * u + UP].rearrange("p (a n) -> p a n", a=2)

            def number(u, heads=(0, 2)):
                lo, hi = heads
                n = hi - lo
                wide = [P, n, TOPK, TOPK]
                pairf = topf[:, 2 * lo:2 * hi].rearrange("p (a r) n -> p a r n", r=2)
                flat = pos[:, lo:hi].rearrange("p a n -> p (a n)")
                cut = slice(TOPK * lo, TOPK * hi)
                step(dve.tensor_scalar(posa[:, cut], flat, 4, None, ALU.logical_shift_right))
                step(dve.tensor_scalar(posb[:, cut], flat, 15, None, ALU.bitwise_and))
                step(dve.tensor_copy(posaf[:, lo:hi].rearrange("p a n -> p (a n)"), posa[:, cut]))
                step(dve.tensor_copy(posbf[:, lo:hi].rearrange("p a n -> p (a n)"), posb[:, cut]))
                for r, (at_, out) in enumerate(((posaf, i0), (posbf, i1))):
                    step(dve.tensor_tensor(hot[:, lo:hi], at_[:, lo:hi].unsqueeze(3).to_broadcast(wide),
                                           iota[:, 0:TOPK].unsqueeze(1).unsqueeze(1).to_broadcast(wide), ALU.is_equal))
                    step(dve.tensor_tensor(hot[:, lo:hi], hot[:, lo:hi],
                                           pairf[:, :, r, :].unsqueeze(2).to_broadcast(wide), ALU.mult))
                    step(dve.tensor_reduce(out[:, cut].rearrange("p (a n) -> p a n", a=n), hot[:, lo:hi], AX.X, ALU.add))
                step(dve.scalar_tensor_tensor(idx[:, UP * u + TOPK * lo:UP * u + TOPK * hi], i0[:, cut], float(NKEYS),
                                              i1[:, cut], ALU.mult, ALU.add))
                dve.sem_inc(idx_ready, n)

            def normalise(u):
                dve.wait_ge(gexp_ready, u + 1)
                step(dve.tensor_reduce(ssum, gates(u), AX.X, ALU.add))
                step(dve.reciprocal(rsum, ssum))
                step(dve.tensor_tensor(gates(u), gates(u), rsum.unsqueeze(2).to_broadcast([P, 2, TOPK]), ALU.mult))

            def products(g, it):
                for k in range(BATCH):
                    if k == 0:
                        dve.wait_ge(gel_ready, it + 1)
                    dve.wait_ge(u_landed[k], 16 * (it + 1))
                    dve.wait_ge(u_free, BATCH * (it + 1) + (k - 1))
                    dve.tensor_tensor_reduce(out=junk4 if k % 2 else junk3, in0=u_rows[k], in1=h[:, g, :], scale=1.0, scalar=0.0,
                                             op0=ALU.mult, op1=ALU.add, accum_out=dots[:, k:k + 1]).then_inc(u_free, 1)

            def weights(it):
                dve.wait_ge(gel_ready, it + 2)
                dve.wait_ge(diag_ready, BATCH * it + 1)
                dve.tensor_tensor(wts[:, 0:BATCH], gel[:, 0:BATCH], gate[:, bass.ds(BATCH * it, BATCH)],
                                  ALU.mult).then_inc(wts_ready, 1)

            def add_experts(g):
                dve.wait_ge(rows_in["g2"], 64)
                for half in range(2):
                    name, cut = f"acc_{g}_{half}", slice(512 * half, 512 * half + 512)
                    wait_filled(dve, name)
                    empties(dve.tensor_tensor(out2[:, cut], bank(name), g2b[:, g, cut], ALU.mult), name)
                    wait_emptied(dve, name)
                    tt(x[:, g, cut], x[:, g, cut], out2[:, cut], ALU.add)
                dve.tensor_tensor_reduce(out=out2, in0=x[:, g, :], in1=x[:, g, :], scale=1.0, scalar=0.0,
                                         op0=ALU.mult, op1=ALU.add, accum_out=ms_f[:, g:g + 1]).then_inc(sqf_ready, 1)
                dve.wait_ge(sqf_ready, g + 1)

            def finish_group(g):
                dve.wait_ge(rstdf_ready, g + 1)
                dve.wait_ge(fn_in, 16)
                dve.scalar_tensor_tensor(h[:, g, :], x[:, g, :], rstd_f[:, g:g + 1], fnb,
                                         ALU.mult, ALU.mult).then_inc(y_out_ready, 1)

            def weigh(g, it):
                products(g, it)
                weights(it)

            dve.sem_inc(u_free, BATCH)
            for head in range(2):
                find(0, (head, head + 1))
                number(0, (head, head + 1))
            products(0, 0)
            normalise(0)
            weights(0)
            find(1)
            number(1)
            products(0, 1)
            normalise(1)
            weights(1)
            find(2)
            number(2)
            normalise(2)
            for u in range(3, UNITS):
                weigh(0, 2 * u - 4)
                find(u)
                weigh(0, 2 * u - 3)
                number(u)
                normalise(u)
            with dve.Fori(2 * (UNITS - 2), NB) as it:
                weigh(0, it)
            with dve.Fori(NB, NB + 2) as it:
                weigh(1, it)
            add_experts(0)
            with dve.Fori(NB + 2, 2 * NB) as it:
                weigh(1, it)
            finish_group(0)
            add_experts(1)
            finish_group(1)


def rope_tables(tokens=P, grid=64, base=10000.0):
    half = ROPE // 2
    inv = (1.0 / (np.float32(base) ** (np.arange(0, half, 2, dtype=np.float32) / np.float32(half)))).astype(np.float32)
    row = (np.arange(tokens) // grid).astype(np.float32)[:, None] * inv
    col = (np.arange(tokens) % grid).astype(np.float32)[:, None] * inv
    ang = np.concatenate([row, row, col, col], axis=-1)
    sign = np.where((np.arange(ROPE) // (ROPE // 4)) % 2 == 0, -1.0, 1.0)
    return np.stack([np.cos(ang), np.sin(ang) * sign], axis=1).astype(np.float32)


def by_state(a):
    a = np.asarray(a)
    lead = a.shape[:-2]
    a = a.reshape(lead + (TILES, 2, SN))
    n = len(lead)
    return np.ascontiguousarray(a.transpose((n + 1, n + 2) + tuple(range(n + 1)))).reshape(P, -1)


def block_diagonal(a):
    a = np.asarray(a).reshape(2, TILES, 2, SN, SP_)
    out = np.zeros((2, SN, 2, TILES, 2, SP_), a.dtype)
    for e in range(2):
        out[e, :, :, :, e, :] = a[:, :, e].transpose(2, 0, 1, 3)
    return out.reshape(P, 2 * TILES, 32)


def kernel(**inputs):
    import concourse.bacc as bacc
    from concourse.bass_utils import run_bass_kernel_spmd as run

    a = {k: np.asarray(v) for k, v in inputs.items()}
    ldt = np.repeat(a["ssm_log_dt"][0][:, :, None], SN, axis=2)
    arrays = {
        "x_prompt": a["x_prompt"][0], "x_sample": a["x_sample"][0],
        "c_cols": np.stack([a["c_ctx"], a["c"][0]], axis=1).reshape(KD, P, G).transpose(1, 0, 2),
        "w_mod": a["w_mod"][0], "b_mod": a["b_mod"][0].reshape(12, 512), "norm1": a["norm1"], "w_in": a["w_in"][0],
        "lam": np.concatenate([by_state(v) for v in (a["ssm_lam_re"][0], a["ssm_lam_im"][0], ldt)], axis=1),
        "bmat": np.stack([block_diagonal(a[k][0]) for k in ("ssm_b_re", "ssm_b_im")], axis=1),
        "cmat": np.stack([block_diagonal(a[k][0].transpose(0, 1, 3, 2)) for k in ("ssm_c_re", "ssm_c_im")], axis=1),
        "ssm_d": a["ssm_d"][0].reshape(NC, P).T,
        "h0": by_state(a["state_ssm"][0, 0].transpose(1, 0, 2, 3)),
        "w_glu": a["w_glu"][0], "q_norm": a["q_norm"], "w_uq": a["w_uq"][0], "kv_norm": a["kv_norm"],
        "w_ukv": np.stack([a["w_uk"][0], a["w_uv"][0]]), "w_out": a["w_out"][0], "norm2": a["norm2"],
        "w_query": a["w_query"][0],
        "keys": a["sub_keys"][0].reshape(HI, NKEYS, P).transpose(2, 0, 1),
        "u_table": a["u_table"][0], "v_table": a["v_table"][0], "final_norm": a["final_norm"][None],
        "cache_ckv": a["cache_ckv"][0, 0], "cache_krope": a["cache_krope"][0, 0],
        "rope_tab": rope_tables(), "ident_in": np.eye(P, dtype=np.float32),
        "iota_in": np.tile(np.arange(P, dtype=np.float32), (P, 1)),
    }
    arrays = {k: np.ascontiguousarray(v) for k, v in arrays.items()}
    outs = {"y_prompt": (P, D), "y_sample": (P, D), "new_ckv": (P, KVR), "new_krope": (P, ROPE), "new_ssm": (2 * 2 * TILES, P)}
    nc = bacc.Bacc("TRN2", target_bir_lowering=False, num_devices=1)
    aps = {k: nc.dram_tensor(k, v.shape, F32, kind="ExternalInput").ap() for k, v in arrays.items()}
    aps |= {k: nc.dram_tensor(k, s, F32, kind="ExternalOutput").ap() for k, s in outs.items()}
    layer(nc, **aps)
    r = run(nc, [arrays], core_ids=[0]).results[0]
    return (r["y_prompt"].reshape(1, P, D), r["y_sample"].reshape(1, P, D), r["new_ckv"].reshape(1, 1, P, KVR),
            r["new_krope"].reshape(1, 1, P, ROPE), r["new_ssm"].reshape(1, 1, 2, 2, SG, SN))
```
